# Optimizing a Trainium2 kernel written in Bass

```python
import math
import jax, jax.numpy as jnp
from jax import lax
import numpy as np

D_MODEL = 1024
BATCH = 1
SEQ = 512
DEPTH = 1
DEC_BATCH = 8
DEC_SEQ = 1
PAST_LEN = 256
PAGE_SIZE = 128

MIX_WIDTH = D_MODEL
SB_WIDTH = MIX_WIDTH // 2
SSM_WIDTH = MIX_WIDTH - SB_WIDTH
SB_HEAD_DIM = 64
SB_HEADS = SB_WIDTH // SB_HEAD_DIM
SB_BIAS_LO = -7.0
SB_BIAS_HI = -4.0
SSM_GROUP = 16
SSM_GROUPS = SSM_WIDTH // SSM_GROUP
SSM_STATE = 64
IN_WIDTH = 3 * SB_WIDTH + SSM_WIDTH
MEM_TOKENS = 256
MEM_HEADS = 4
MEM_HEAD_DIM = D_MODEL // MEM_HEADS
D_FF = ((8 * D_MODEL // 3 + 127) // 128) * 128
CONV_W = 3
BLOCK_Q = 128
EPS = 1e-6
DT_MIN = 1e-3
DT_MAX = 1e-1

kernel_name = "hymba_s5_stickbreaking_memxattn_convffn_step"

def _rmsnorm(x, g):
    xf = x.astype(jnp.float32)
    y = xf * lax.rsqrt(jnp.mean(xf * xf, axis=-1, keepdims=True) + EPS)
    return (y * g.astype(jnp.float32)).astype(x.dtype)

def _sb_block(q_blk, q_pos, k, v, k_pos, sb_bias):
    z = jnp.einsum('bqhd,bkhd->bhqk', q_blk.astype(jnp.float32), k.astype(jnp.float32)) / math.sqrt(SB_HEAD_DIM)
    z = z + sb_bias.astype(jnp.float32)[None, :, None, None]
    causal = k_pos[None, :] < q_pos[:, None]
    log_not_beta = jnp.where(causal, -jax.nn.softplus(z), 0.0)
    after = lax.cumsum(log_not_beta, axis=3, reverse=True) - log_not_beta
    a = jnp.where(causal, jnp.exp(jax.nn.log_sigmoid(z) + after), 0.0)
    return jnp.einsum('bhqk,bkhd->bqhd', a, v.astype(jnp.float32)).astype(v.dtype)

def _stick_breaking(q, k, v, q_pos, k_pos, sb_bias):
    b, n_q, h, dh = q.shape
    if n_q > BLOCK_Q and n_q % BLOCK_Q == 0:
        n_blk = n_q // BLOCK_Q
        qb = q.reshape(b, n_blk, BLOCK_Q, h, dh).transpose(1, 0, 2, 3, 4)
        pb = q_pos.reshape(n_blk, BLOCK_Q)
        out = lax.map(lambda a: _sb_block(a[0], a[1], k, v, k_pos, sb_bias), (qb, pb))
        return out.transpose(1, 0, 2, 3, 4).reshape(b, n_q, h, dh)
    return _sb_block(q, q_pos, k, v, k_pos, sb_bias)

def _s5(u, h0, lam_re, lam_im, log_dt, b_re, b_im, c_re, c_im, d_skip, w_glu, b_glu):
    bsz, t = u.shape[:2]
    ug = u.astype(jnp.float32).reshape(bsz, t, SSM_GROUPS, SSM_GROUP)
    lam = lax.complex(lam_re.astype(jnp.float32), lam_im.astype(jnp.float32))
    dt = jnp.exp(log_dt.astype(jnp.float32))[:, None]
    lam_bar = jnp.exp(lam * dt)
    bmat = lax.complex(b_re.astype(jnp.float32), b_im.astype(jnp.float32))
    cmat = lax.complex(c_re.astype(jnp.float32), c_im.astype(jnp.float32))
    b_bar = ((lam_bar - 1.0) / lam)[..., None] * bmat
    bu = jnp.einsum('gnp,btgp->btgn', b_bar, ug)
    bu = bu.at[:, 0].add(lam_bar * h0)
    decay = jnp.broadcast_to(lam_bar, bu.shape)

    def combine(e1, e2):
        a1, x1 = e1
        a2, x2 = e2
        return a2 * a1, a2 * x1 + x2

    _, hs = lax.associative_scan(combine, (decay, bu), axis=1)
    y = jnp.einsum('gpn,btgn->btgp', cmat, hs).real + d_skip.astype(jnp.float32).reshape(SSM_GROUPS, SSM_GROUP) * ug
    y = jax.nn.gelu(y.reshape(bsz, t, SSM_WIDTH))
    out = y * jax.nn.sigmoid(y @ w_glu.astype(jnp.float32) + b_glu.astype(jnp.float32))
    return out.astype(u.dtype), hs[:, -1]

def _mem_kv(mem, g_mem_kv, w_mk, w_mv):
    b = mem.shape[0]
    m = _rmsnorm(mem, g_mem_kv)
    mk = (m @ w_mk).reshape(b, MEM_TOKENS, MEM_HEADS, MEM_HEAD_DIM)
    mv = (m @ w_mv).reshape(b, MEM_TOKENS, MEM_HEADS, MEM_HEAD_DIM)
    return mk, mv

def _mem_attend(h, mk, mv, w_mq, w_mo):
    b, t, _ = h.shape
    q = (h @ w_mq).reshape(b, t, MEM_HEADS, MEM_HEAD_DIM)
    s = jnp.einsum('bqhd,bkhd->bhqk', q.astype(jnp.float32), mk.astype(jnp.float32)) / math.sqrt(MEM_HEAD_DIM)
    p = jax.nn.softmax(s, axis=-1)
    o = jnp.einsum('bhqk,bkhd->bqhd', p, mv.astype(jnp.float32)).reshape(b, t, D_MODEL)
    return o.astype(h.dtype) @ w_mo

def _conv_ffn(h, prev, w_gate, w_up, conv_w, conv_b, w_down):
    t = h.shape[1]
    gate_in = h @ w_gate
    buf = jnp.concatenate([prev.astype(gate_in.dtype), gate_in], axis=1)
    conv = conv_b
    for j in range(CONV_W):
        conv = conv + conv_w[j] * buf[:, j:j + t]
    out = (jax.nn.gelu(conv) * (h @ w_up)) @ w_down
    return out, buf[:, -(CONV_W - 1):]

def _layer(x, k_past, v_past, past_len, h0, conv_prev, mem_k, mem_v, lp):
    b, t, _ = x.shape
    h = _rmsnorm(x, lp['g_mix'])
    proj = h @ lp['w_in']
    q, k, v, u = jnp.split(proj, [SB_WIDTH, 2 * SB_WIDTH, 3 * SB_WIDTH], axis=-1)
    q = q.reshape(b, t, SB_HEADS, SB_HEAD_DIM)
    k = k.reshape(b, t, SB_HEADS, SB_HEAD_DIM)
    v = v.reshape(b, t, SB_HEADS, SB_HEAD_DIM)
    q_pos = past_len + jnp.arange(t, dtype=jnp.int32)
    if k_past is None:
        k_all, v_all, k_pos = k, v, q_pos
    else:
        k_all = jnp.concatenate([k_past.astype(k.dtype), k], axis=1)
        v_all = jnp.concatenate([v_past.astype(v.dtype), v], axis=1)
        k_pos = jnp.arange(past_len + t, dtype=jnp.int32)
    o_sb = _stick_breaking(q, k_all, v_all, q_pos, k_pos, lp['sb_bias']).reshape(b, t, SB_WIDTH)
    o_ssm, h_last = _s5(u, h0, lp['lam_re'], lp['lam_im'], lp['log_dt'], lp['b_re'], lp['b_im'],
                        lp['c_re'], lp['c_im'], lp['d_skip'], lp['w_glu'], lp['b_glu'])
    mix = jnp.concatenate([_rmsnorm(o_sb, lp['g_sb_out']), _rmsnorm(o_ssm, lp['g_ssm_out'])], axis=-1)
    x = x + mix @ lp['w_out']
    x = x + _mem_attend(_rmsnorm(x, lp['g_mem_q']), mem_k, mem_v, lp['w_mq'], lp['w_mo'])
    f, conv_state = _conv_ffn(_rmsnorm(x, lp['g_ffn']), conv_prev, lp['w_gate'], lp['w_up'],
                              lp['conv_w'], lp['conv_b'], lp['w_down'])
    x = x + f
    return x, k, v, h_last, conv_state

def setup_inputs(seed: int = 0) -> dict:
    key = jax.random.key(seed)
    ks = iter(jax.random.split(key, 48))
    f32 = jnp.float32

    def nrm(shape, scale):
        return jax.random.normal(next(ks), shape, f32) * scale

    def gain(shape):
        return 1.0 + nrm(shape, 0.02)

    n_pages = PAST_LEN // PAGE_SIZE
    n_pool = (DEC_BATCH * n_pages * 5) // 4
    L = DEPTH
    inp = {}
    inp['x_prompt'] = nrm((BATCH, SEQ, D_MODEL), 1.0)
    inp['x_sample'] = nrm((DEC_BATCH, DEC_SEQ, D_MODEL), 1.0)
    inp['cache_sb_k'] = nrm((L, n_pool, PAGE_SIZE, SB_HEADS, SB_HEAD_DIM), 1.0)
    inp['cache_sb_v'] = nrm((L, n_pool, PAGE_SIZE, SB_HEADS, SB_HEAD_DIM), 1.0)
    perm = jax.random.permutation(next(ks), n_pool)[:DEC_BATCH * n_pages]
    inp['page_table'] = perm.reshape(DEC_BATCH, n_pages).astype(jnp.int32)
    inp['state_ssm_re'] = nrm((L, DEC_BATCH, SSM_GROUPS, SSM_STATE), 0.5)
    inp['state_ssm_im'] = nrm((L, DEC_BATCH, SSM_GROUPS, SSM_STATE), 0.5)
    inp['state_conv'] = nrm((L, DEC_BATCH, CONV_W - 1, D_FF), 1.0)
    inp['cache_mem_k'] = nrm((L, DEC_BATCH, MEM_TOKENS, MEM_HEADS, MEM_HEAD_DIM), 1.0)
    inp['cache_mem_v'] = nrm((L, DEC_BATCH, MEM_TOKENS, MEM_HEADS, MEM_HEAD_DIM), 1.0)
    inp['mem_prompt'] = nrm((BATCH, MEM_TOKENS, D_MODEL), 1.0)
    inp['g_mix'] = gain((L, D_MODEL))
    inp['w_in'] = nrm((L, D_MODEL, IN_WIDTH), D_MODEL ** -0.5)
    inp['sb_bias'] = jax.random.uniform(next(ks), (L, SB_HEADS), f32, SB_BIAS_LO, SB_BIAS_HI)
    inp['lam_re'] = -0.5 + nrm((L, SSM_GROUPS, SSM_STATE), 0.01)
    inp['lam_im'] = math.pi * jnp.arange(SSM_STATE, dtype=f32) + nrm((L, SSM_GROUPS, SSM_STATE), 0.01)
    inp['log_dt'] = jax.random.uniform(next(ks), (L, SSM_GROUPS), f32, math.log(DT_MIN), math.log(DT_MAX))
    inp['b_re'] = nrm((L, SSM_GROUPS, SSM_STATE, SSM_GROUP), (2 * SSM_GROUP) ** -0.5)
    inp['b_im'] = nrm((L, SSM_GROUPS, SSM_STATE, SSM_GROUP), (2 * SSM_GROUP) ** -0.5)
    inp['c_re'] = nrm((L, SSM_GROUPS, SSM_GROUP, SSM_STATE), (2 * SSM_STATE) ** -0.5)
    inp['c_im'] = nrm((L, SSM_GROUPS, SSM_GROUP, SSM_STATE), (2 * SSM_STATE) ** -0.5)
    inp['d_skip'] = nrm((L, SSM_WIDTH), 1.0)
    inp['w_glu'] = nrm((L, SSM_WIDTH, SSM_WIDTH), SSM_WIDTH ** -0.5)
    inp['b_glu'] = nrm((L, SSM_WIDTH), 0.01)
    inp['g_sb_out'] = gain((L, SB_WIDTH))
    inp['g_ssm_out'] = gain((L, SSM_WIDTH))
    inp['w_out'] = nrm((L, MIX_WIDTH, D_MODEL), MIX_WIDTH ** -0.5)
    inp['g_mem_q'] = gain((L, D_MODEL))
    inp['g_mem_kv'] = gain((L, D_MODEL))
    inp['w_mq'] = nrm((L, D_MODEL, D_MODEL), D_MODEL ** -0.5)
    inp['w_mk'] = nrm((L, D_MODEL, D_MODEL), D_MODEL ** -0.5)
    inp['w_mv'] = nrm((L, D_MODEL, D_MODEL), D_MODEL ** -0.5)
    inp['w_mo'] = nrm((L, D_MODEL, D_MODEL), D_MODEL ** -0.5)
    inp['g_ffn'] = gain((L, D_MODEL))
    inp['w_gate'] = nrm((L, D_MODEL, D_FF), D_MODEL ** -0.5)
    inp['w_up'] = nrm((L, D_MODEL, D_FF), D_MODEL ** -0.5)
    inp['conv_w'] = nrm((L, CONV_W, D_FF), CONV_W ** -0.5)
    inp['conv_b'] = nrm((L, D_FF), 0.01)
    inp['w_down'] = nrm((L, D_FF, D_MODEL), D_FF ** -0.5)
    inp['g_final'] = gain((D_MODEL,))
    return inp

def reference(x_prompt, x_sample, cache_sb_k, cache_sb_v, page_table, state_ssm_re, state_ssm_im,
              state_conv, cache_mem_k, cache_mem_v, mem_prompt,
              g_mix, w_in, sb_bias, lam_re, lam_im, log_dt, b_re, b_im, c_re, c_im, d_skip, w_glu, b_glu,
              g_sb_out, g_ssm_out, w_out, g_mem_q, g_mem_kv, w_mq, w_mk, w_mv, w_mo,
              g_ffn, w_gate, w_up, conv_w, conv_b, w_down, g_final):
    n_p = x_prompt.shape[0]
    n_s = x_sample.shape[0]
    past_len = page_table.shape[1] * cache_sb_k.shape[2]
    yp, ys = x_prompt, x_sample
    pk, pv, pre, pim, pconv, pmk, pmv = [], [], [], [], [], [], []
    sk, sv, sre, sim, sconv = [], [], [], [], []
    for l in range(DEPTH):
        lp = dict(g_mix=g_mix[l], w_in=w_in[l], sb_bias=sb_bias[l], lam_re=lam_re[l], lam_im=lam_im[l],
                  log_dt=log_dt[l], b_re=b_re[l], b_im=b_im[l], c_re=c_re[l], c_im=c_im[l], d_skip=d_skip[l],
                  w_glu=w_glu[l], b_glu=b_glu[l], g_sb_out=g_sb_out[l], g_ssm_out=g_ssm_out[l],
                  w_out=w_out[l], g_mem_q=g_mem_q[l], w_mq=w_mq[l], w_mo=w_mo[l], g_ffn=g_ffn[l],
                  w_gate=w_gate[l], w_up=w_up[l], conv_w=conv_w[l], conv_b=conv_b[l], w_down=w_down[l])
        mk_p, mv_p = _mem_kv(mem_prompt, g_mem_kv[l], w_mk[l], w_mv[l])
        h0_p = jnp.zeros((n_p, SSM_GROUPS, SSM_STATE), jnp.complex64)
        conv0 = jnp.zeros((n_p, CONV_W - 1, D_FF), yp.dtype)
        yp, kp, vp, hp, cp = _layer(yp, None, None, 0, h0_p, conv0, mk_p, mv_p, lp)
        pk.append(kp); pv.append(vp); pconv.append(cp); pmk.append(mk_p); pmv.append(mv_p)
        pre.append(hp.real); pim.append(hp.imag)
        k_past = cache_sb_k[l][page_table].reshape(n_s, past_len, SB_HEADS, SB_HEAD_DIM)
        v_past = cache_sb_v[l][page_table].reshape(n_s, past_len, SB_HEADS, SB_HEAD_DIM)
        h0_s = lax.complex(state_ssm_re[l].astype(jnp.float32), state_ssm_im[l].astype(jnp.float32))
        ys, ks_, vs_, hs_, cs_ = _layer(ys, k_past, v_past, past_len, h0_s, state_conv[l],
                                        cache_mem_k[l], cache_mem_v[l], lp)
        sk.append(ks_); sv.append(vs_); sconv.append(cs_)
        sre.append(hs_.real); sim.append(hs_.imag)
    y_prompt = _rmsnorm(yp, g_final)
    y_sample = _rmsnorm(ys, g_final)
    return (y_prompt, y_sample,
            jnp.stack(pk), jnp.stack(pv), jnp.stack(pre), jnp.stack(pim), jnp.stack(pconv),
            jnp.stack(pmk), jnp.stack(pmv),
            jnp.stack(sk), jnp.stack(sv), jnp.stack(sre), jnp.stack(sim), jnp.stack(sconv))


_drawn_inputs = setup_inputs


def setup_inputs(seed=0):
    import zlib

    import numpy as np

    out = dict(_drawn_inputs(seed))
    spreads = {}
    factors = {'lam_re': 59.538,
     'b_glu': 8.0,
     'g_sb_out': 5.201,
     'g_ssm_out': 5.114,
     'g_mem_q': 8.0,
     'g_mem_kv': 2.748,
     'g_ffn': 8.232,
     'conv_b': 27.445,
     'g_final': 20.079}
    for name, (base, spread) in spreads.items():
        noise = np.random.default_rng([zlib.crc32(name.encode()), seed]).standard_normal(out[name].shape)
        drawn = base * np.exp(spread * noise) if base else spread * noise
        out[name] = __import__('jax').numpy.asarray(drawn.astype(out[name].dtype))
    for name, factor in factors.items():
        out[name] = (out[name] * factor).astype(out[name].dtype)
    return out
```

```python
from contextlib import ExitStack, contextmanager

import numpy as np

import concourse.bass as bass
from concourse import mybir

F32 = mybir.dt.float32
F32R = mybir.dt.float32r
I32 = mybir.dt.int32
ALU = mybir.AluOpType
ACT = mybir.ActivationFunctionType
AX = mybir.AxisListType

P = 128
D = 1024
KT = D // P
TP = 512
NS = 8
T = TP + NS
HALF = T // 2
EPS = 1e-6
SBW = 512
AT = SBW // P
HEADS = 8
DH = 64
PAGES = 2
PAIRS = 16
GP = 32
CH = 4
NCH = TP // CH
MT = 256
MH = 4
ROWS = NS * MH
FF = 2816
FT = FF // P
DOWN_CHUNKS = (8, 8, 6)

N_U, N_Q, N_K, N_V, N_GLU, N_MK, N_MV, N_OUT, N_MQ, N_MO, N_GU, N_DOWN, N_END = (
    0, 4, 8, 12, 16, 18, 26, 34, 42, 50, 58, 102, 126)

_widths = dict(g_mix=8, g_mem_q=8, g_mem_kv=8, g_ffn=8, g_final=8, g_sb=4, g_ssm=4, b_glu=4,
               conv_w0=FT, conv_w1=FT, conv_w2=FT, conv_b=FT, sb_bias=HEADS,
               lam_re=PAIRS, lam_im=PAIRS, log_dt=PAIRS, h0_re=PAIRS * NS, h0_im=PAIRS * NS,
               conv_prev=FT * 2 * NS)
COL = {}
_at = 0
for _name, _width in _widths.items():
    COL[_name] = _at
    _at += _width
NCOL = _at

TWO_PI_INV = float(np.float32(1.0 / (2.0 * np.pi)))
ROUND = 12582912.0
TWO_PI_A = 6.28125
TWO_PI_B = 0.0019350051879882812
TWO_PI_C = float(2.0 * np.pi - 6.28125 - 0.0019350051879882812)
HALF_PI = float(np.pi / 2)
PI_IN = 3.1415925


class Order:

    def __init__(self, eng, sem):
        self.eng, self.sem, self.count = eng, sem, 0

    def done(self, ins):
        ins.then_inc(self.sem, 1)
        self.count = self.count + 1
        self.eng.wait_ge(self.sem, self.count)

    @contextmanager
    def loop(self, turns, per_turn):
        start = self.count
        with self.eng.Fori(0, turns) as i:
            self.count = i * per_turn + start
            yield i
        self.count = start + turns * per_turn


def build(nc, xT, memT, wblk, cols_d, bc_d, dskip_d, consts_d, pages_d, kpool, vpool, kmem, vmem,
          conv_prev_rows,
          y_out, k_out, v_out, vs_out, ssm_out_d, gate_out, conv_s0_out, mk_out, mv_out):
    ctx = ExitStack()
    s5ctx, midctx, xctx, ffctx, sbctx = (ExitStack() for _ in range(5))

    def sem(name):
        return ctx.enter_context(nc.semaphore(name))

    def sbuf(where, name, shape, dt=F32):
        return where.enter_context(nc.sbuf_tensor(name, shape, dt))

    with ctx:
        w_raw = sbuf(ctx, "w_raw", [P, 4, 1024])
        w_hi = sbuf(ctx, "w_hi", [P, 2, 1024], F32R)
        w_lo = sbuf(ctx, "w_lo", [P, 2, 1024], F32R)
        x = sbuf(ctx, "x", [P, KT, T])
        h_hi = sbuf(ctx, "h_hi", [P, KT, T], F32R)
        h_lo = sbuf(ctx, "h_lo", [P, KT, T], F32R)
        consts = sbuf(ctx, "consts", [P, 4, P])
        ident, ntri, nones, ones = (consts[:, i, :] for i in range(4))
        cols = sbuf(ctx, "cols", [P, NCOL])
        rinv = sbuf(ctx, "rinv", [P, T])
        rinv_col = sbuf(ctx, "rinv_col", [P, 5])
        acc = sbuf(ctx, "acc", [P, T])
        sq = sbuf(ctx, "sq", [P, T])
        cap = sbuf(ctx, "cap", [P, HEADS])
        page_ids = sbuf(ctx, "page_ids", [1, NS * PAGES], I32)
        ssm_out = sbuf(ctx, "ssm_out", [P, 2, PAIRS, NS + 1])
        qT = sbuf(sbctx, "qT", [P, AT, T])
        kT = sbuf(sbctx, "kT", [P, AT, T])
        vtok = sbuf(sbctx, "vtok", [P, 4, SBW])
        w2re = sbuf(s5ctx, "w2re", [P, PAIRS, P])
        w2im = sbuf(s5ctx, "w2im", [P, PAIRS, P])
        qre = sbuf(s5ctx, "qre", [P, PAIRS, CH, GP])
        qim = sbuf(s5ctx, "qim", [P, PAIRS, CH, GP])
        mt = sbuf(s5ctx, "mt", [P, PAIRS, P])
        u2 = sbuf(s5ctx, "u2", [P, PAIRS, NCH])
        u_first = sbuf(s5ctx, "u_first", [P, PAIRS, NS])
        u_last = sbuf(s5ctx, "u_last", [P, PAIRS, NS])
        ere = sbuf(s5ctx, "ere", [P, PAIRS, NCH])
        eim = sbuf(s5ctx, "eim", [P, PAIRS, NCH])
        sre = sbuf(s5ctx, "sre", [P, PAIRS * (NCH + 1)])
        sim = sbuf(s5ctx, "sim", [P, PAIRS * (NCH + 1)])
        cmat = sbuf(s5ctx, "cmat", [P, 2, PAIRS, GP])
        q_tmp = sbuf(s5ctx, "q_tmp", [P, PAIRS, GP])
        sm = sbuf(s5ctx, "sm", [P, 34, PAIRS])
        s5ctx.close()
        bmat = ere[:, :, :].rearrange("p k c -> p (k c)")[:, 0:1024].rearrange(
            "p (a k g) -> p a k g", a=2, k=PAIRS)
        ncim = ere[:, :, :].rearrange("p k c -> p (k c)")[:, 1024:1536].rearrange("p (k g) -> p k g", k=PAIRS)
        dskip = ere[:, :, :].rearrange("p k c -> p (k c)")[:, 1536:2048].rearrange("p (k g) -> p k g", k=PAIRS)
        wtre = sre[:, 0:PAIRS * P].rearrange("p (k j g) -> p k j g", k=PAIRS, j=CH)
        wtim = sim[:, 0:PAIRS * P].rearrange("p (k j g) -> p k j g", k=PAIRS, j=CH)
        sre3 = sre[:, :].rearrange("p (k c) -> p k c", k=PAIRS)
        sim3 = sim[:, :].rearrange("p (k c) -> p k c", k=PAIRS)
        uT = kT
        vs = w2re[0:NS, 0:4, :].rearrange("p k s -> p (k s)")
        tmp = vtok
        mkT = sbuf(midctx, "mkT", [P, KT, MT])
        mv = sbuf(midctx, "mv", [P, 2, D])
        memx = mv[:, :, :].rearrange("p a (b t) -> p (a b) t", t=MT)
        att = ExitStack()
        sp = sbuf(att, "sp", [P, 2, 1920])
        osb = sbuf(att, "osb", [P, AT, T])
        yT = sbuf(att, "yT", [P, AT, T])
        m_hi = sbuf(att, "m_hi", [P, KT, MT], F32R)
        m_lo = sbuf(att, "m_lo", [P, KT, MT], F32R)
        kpg = sbuf(att, "kpg", [P, 4, SBW])
        vpg = sbuf(att, "vpg", [P, 4, SBW])
        qbd = sbuf(att, "qbd", [P, AT, NS, 2])
        dz = sbuf(att, "dz", [P, 4, PAGES * NS * HEADS])
        rinv_m = sbuf(att, "rinv_m", [P, MT])
        att.close()
        qm = sbuf(xctx, "qm", [P, KT, T])
        prob = sbuf(xctx, "prob", [P, 2, 4, MT])
        probT = sbuf(xctx, "probT", [P, 2, TP])
        stat = sbuf(xctx, "stat", [P, 2, 3, 4])
        kmd = sbuf(xctx, "kmd", [P, 3, KT * MT])
        vmd = sbuf(xctx, "vmd", [P, 2, 2 * D])
        drow = sbuf(xctx, "drow", [ROWS, MT])
        dstat = sbuf(xctx, "dstat", [ROWS, 4])
        xctx.close()
        qz = [t[:, :, :].rearrange("p a t -> p (a t)")[:, 0:4 * ROWS * (NS + 1)].rearrange(
            "p (f c) -> p f c", f=4) for t in (qT, kT)]
        pz = vtok[:, :, :].rearrange("p a (c w) -> p (a c) w", w=ROWS).rearrange(
            "p (t c) w -> p t c w", t=2)
        midctx.close()
        sbctx.close()
        a_hi = sbuf(ffctx, "a_hi", [P, FT, T], F32R)
        a_lo = sbuf(ffctx, "a_lo", [P, FT, T], F32R)
        gate = sbuf(ffctx, "gate", [P, 2, T + 2])
        conv = sbuf(ffctx, "conv", [P, 2, T])
        gate_keep = sbuf(ffctx, "gate_keep", [P, FT, 2 + NS])
        ffctx.close()

        pj = ctx.enter_context(nc.psum_tensor("pj", [P, 4, 512], F32))
        aux = ctx.enter_context(nc.psum_tensor("aux", [P, 4, 512], F32))

        x_loaded = [sem(f"x_loaded{i}") for i in range(4)]
        cols_loaded = sem("cols_loaded")
        s5_loaded = sem("s5_loaded")
        consts_loaded = sem("consts_loaded")
        pages_loaded = sem("pages_loaded")
        mem_loaded = sem("mem_loaded")
        raw_loaded = [sem(f"raw_loaded{i}") for i in range(4)]
        kpg_loaded = [sem(f"kpg_loaded{i}") for i in range(4)]
        vpg_loaded = [sem(f"vpg_loaded{i}") for i in range(4)]
        kmd_loaded = [sem(f"kmd_loaded{i}") for i in range(3)]
        vmd_loaded = [sem(f"vmd_loaded{i}") for i in range(2)]
        kv_stored = sem("kv_stored")
        stored = sem("stored")
        hi_done = sem("hi_done")
        lo_done = sem("lo_done")
        block_done = sem("block_done")
        evacuated = sem("evacuated")
        h_hi_done = sem("h_hi_done")
        h_split = sem("h_split")
        sq_ready = sem("sq_ready")
        acc_added = sem("acc_added")
        stats_done = sem("stats_done")
        root_done = sem("root_done")
        rinv_done = sem("rinv_done")
        dve_order = sem("dve_order")
        act_order = sem("act_order")
        pool_order = sem("pool_order")
        dt_done = sem("dt_done")
        angle_done = sem("angle_done")
        polar_done = sem("polar_done")
        powers_done = sem("powers_done")
        wt_built = sem("wt_built")
        negc_done = sem("negc_done")
        wt_turned = sem("wt_turned")
        w2_copied = sem("w2_copied")
        kernel_done = sem("kernel_done")
        mt_zeroed = sem("mt_zeroed")
        mt_built = sem("mt_built")
        k0_added = sem("k0_added")
        u_zeroed = sem("u_zeroed")
        u2_act = sem("u2_act")
        u2_dve = sem("u2_dve")
        q_built = sem("q_built")
        v_done = sem("v_done")
        v_read = sem("v_read")
        vtail_read = sem("vtail_read")
        vs_done = sem("vs_done")
        vs_read = sem("vs_read")
        states_done = sem("states_done")
        ssm_out_done = sem("ssm_out_done")
        y_done = sem("y_done")
        gelu_done = sem("gelu_done")
        y_hi_done = sem("y_hi_done")
        y_split = sem("y_split")
        qk_done = sem("qk_done")
        capped = sem("capped")
        soft_log = sem("soft_log")
        soft_done = sem("soft_done")
        soft_masked = sem("soft_masked")
        cum_done = sem("cum_done")
        a_exp = sem("a_exp")
        a_masked = sem("a_masked")
        av_done = sem("av_done")
        o_read = sem("o_read")
        qbd_ready = sem("qbd_ready")
        dscore_pg = sem("dscore_pg")
        dsoft_log = sem("dsoft_log")
        dz_ready = sem("dz_ready")
        dsp_ready = sem("dsp_ready")
        dcum_done = sem("dcum_done")
        da_arg = sem("da_arg")
        da_ready = sem("da_ready")
        dav_pg = sem("dav_pg")
        dav_read = sem("dav_read")
        m_scaled = sem("m_scaled")
        m_hi_done = sem("m_hi_done")
        m_split = sem("m_split")
        sig_done = sem("sig_done")
        mix_scaled = sem("mix_scaled")
        s_done = sem("s_done")
        smax_done = sem("smax_done")
        p_exp = sem("p_exp")
        p_ready = sem("p_ready")
        pt_done = sem("pt_done")
        pt_copied = sem("pt_copied")
        o_done = sem("o_done")
        o_hi = sem("o_hi")
        o_lo = sem("o_lo")
        kmd_used = sem("kmd_used")
        drow_max = sem("drow_max")
        drow_exp = sem("drow_exp")
        drow_ready = sem("drow_ready")
        dp_turned = sem("dp_turned")
        dp_copied = sem("dp_copied")
        vmd_used = sem("vmd_used")
        z_cleared = sem("z_cleared")
        qz_ready = sem("qz_ready")
        do_rows = sem("do_rows")
        do_turned = sem("do_turned")
        do_hi = sem("do_hi")
        do_lo = sem("do_lo")
        gate_pads = sem("gate_pads")
        tap2_done = sem("tap2_done")
        conv_done = sem("conv_done")
        ff_gelu = sem("ff_gelu")
        a_hi_done = sem("a_hi_done")
        a_split = sem("a_split")
        y_scaled = sem("y_scaled")

        def col(name, i=0, n=1):
            return cols[:, COL[name] + i:COL[name] + i + n]

        def h0(part, k):
            return col("h0_im" if part else "h0_re", NS * k, NS)

        def halves(ap):
            return ap.rearrange("p (a t) -> p a t", a=2)

        def slot(e):
            return pj[:, 2 * (e % 2):2 * (e % 2) + 2, 0:HALF]

        def raw_count(n, i=0, step=4):
            return 16 * (n // 4 + 1) + i * (16 * step // 4)

        REGION = [(0, 0, 512), (1, 128, 512), (2, 256, 512), (1, 0, 128)]

        def at(h, i, q0):
            bank, a, b = REGION[i]
            t = aux if h % 2 == 0 else pj
            return t[:, bank, a + q0 - 128 * i:b]

        def sp_at(h, i, q0):
            bank, a, b = REGION[i]
            return sp[:, h % 2, 512 * bank + a + q0 - 128 * i:512 * bank + b]

        def spans(h):
            t = aux if h % 2 == 0 else pj
            flat = t[:, :, :].rearrange("p b c -> p (b c)")
            return [(flat[:, a:b], sp[:, h % 2, a:b]) for a, b in ((0, 1024), (1280, 1536))]

        def o_bank(pair):
            return (aux if pair % 2 == 0 else pj)[:, 3, :]

        block = ctx.enter_context(nc.Block())

        @block.sync
        def _(sp_eng):
            eng = sp_eng

            def load_block(n):
                if n >= 4:
                    eng.wait_ge(lo_done, n - 3)
                eng.dma_start(w_raw[:, n % 4, :], wblk[n]).then_inc(raw_loaded[n % 4], 16)

            def load_blocks(first, last):
                with eng.Fori(0, (last - first) // 4) as i:
                    for s in range(4):
                        eng.wait_ge(lo_done, first + s - 3 + i * 4)
                        eng.dma_start(w_raw[:, (first + s) % 4, :], wblk[i * 4 + (first + s)]).then_inc(
                            raw_loaded[(first + s) % 4], 16)

            eng.dma_start(cols[:, :], cols_d).then_inc(cols_loaded, 16)
            for c in range(4):
                eng.dma_start(x[:, 2 * c:2 * c + 2, :], xT[:, 2 * c:2 * c + 2, :]).then_inc(x_loaded[c], 16)
                load_block(c)
            eng.dma_start(bmat, bc_d[:, 0:2]).then_inc(s5_loaded, 16)
            eng.dma_start(cmat[:, :, :, :], bc_d[:, 2:4]).then_inc(s5_loaded, 16)
            eng.dma_start(dskip[96:128], dskip_d).then_inc(s5_loaded, 16)
            eng.dma_start(consts[:, :, :], consts_d).then_inc(consts_loaded, 16)
            eng.dma_start(page_ids[:, :], pages_d).then_inc(pages_loaded, 16)
            eng.dma_start(conv_s0_out, conv_prev_rows).then_inc(stored, 16)
            load_blocks(4, 20)
            eng.wait_ge(evacuated, 16)
            eng.dma_start(k_out, kT[:, :, :]).then_inc(kv_stored, 16)
            eng.dma_start(v_out, vtok[:, :, :]).then_inc(kv_stored, 16)
            eng.dma_start(vs_out, vs).then_inc(kv_stored, 16)
            eng.wait_ge(ssm_out_done, 2)
            eng.dma_start(ssm_out_d, ssm_out[:, :, :, :]).then_inc(stored, 16)
            eng.wait_ge(y_done, 5)
            eng.dma_start(memx, memT).then_inc(mem_loaded, 16)
            eng.wait_ge(pages_loaded, 16)

            def load_page(n, tile, pool, loaded):
                page = eng.value_load(page_ids[0:1, n:n + 1], min_val=0, max_val=pool.shape[0] - 1)
                eng.dma_start(tile[:, n % 4, :], pool[bass.ds(page, 1)].rearrange("a p n -> (a p) n")).then_inc(
                    loaded[n % 4], 16)

            for n in range(4):
                load_page(n, kpg, kpool, kpg_loaded)
                load_page(n, vpg, vpool, vpg_loaded)
            for n in range(4, NS * PAGES):
                eng.wait_ge(dscore_pg, n - 3)
                load_page(n, kpg, kpool, kpg_loaded)
            load_block(20)
            load_block(21)
            for n in range(4, NS * PAGES):
                eng.wait_ge(dav_pg, n - 3)
                load_page(n, vpg, vpool, vpg_loaded)
            load_blocks(22, 42)
            eng.wait_ge(evacuated, N_OUT + 2)
            eng.dma_start(mk_out, mkT[:, :, :]).then_inc(stored, 16)
            eng.dma_start(mv_out, mv[:, :, :]).then_inc(stored, 16)
            eng.wait_ge(block_done, N_OUT)
            eng.wait_ge(h_split, 16)

            def load_kmem(b):
                eng.dma_start(kmd[:, b % 3, :], kmem[b]).then_inc(kmd_loaded[b % 3], 16)

            def load_vmem(b):
                eng.dma_start(vmd[:, b % 2, :], vmem[b]).then_inc(vmd_loaded[b % 2], 16)

            for b in range(3):
                load_kmem(b)
            for b in range(2):
                load_vmem(b)
            load_blocks(42, 54)
            for b in range(3, NS):
                eng.wait_ge(kmd_used, b - 2)
                load_kmem(b)
            for b in range(2, NS):
                eng.wait_ge(vmd_used, b - 1)
                load_vmem(b)
            load_blocks(54, 126)
            eng.wait_ge(a_split, FT)
            eng.dma_start(gate_out, gate_keep[:, :, :]).then_inc(stored, 16)
            for kt in range(KT):
                eng.wait_ge(y_scaled, kt + 1)
                eng.dma_start(y_out[:, kt, :], x[:, kt, :]).then_inc(stored, 16)
            eng.wait_ge(kv_stored, 16 * 3)
            eng.wait_ge(stored, 16 * 13)

        @block.gpsimd
        def _(pool):
            order = Order(pool, pool_order)

            def low(n, i=0):
                pool.wait_ge(hi_done, n + 1 + i * 4)
                nc.gpsimd.tensor_tensor(w_lo[:, n % 2, :], w_raw[:, n % 4, :], w_hi[:, n % 2, :].bitcast(F32),
                                        ALU.subtract).then_inc(lo_done, 1)

            nc.gpsimd.memset(u_first[:, :, :], 0.0)
            nc.gpsimd.memset(u_last[:, :, :], 0.0).then_inc(u_zeroed, 1)
            nc.gpsimd.memset(mt[:, :, :], 0.0).then_inc(mt_zeroed, 1)
            low(0)
            low(1)
            low(2)
            pool.wait_ge(powers_done, 1)
            pool.wait_ge(s5_loaded, 48)
            for i in range(CH):
                lre = sm[:, 2 * i, :].unsqueeze(2).broadcast_to([P, PAIRS, GP])
                lim = sm[:, 2 * i + 1, :].unsqueeze(2).broadcast_to([P, PAIRS, GP])
                cre, cim = cmat[:, 0], cmat[:, 1]
                qr, qi = qre[:, :, i, :], qim[:, :, i, :]
                t = q_tmp[:, :, :]
                nc.gpsimd.tensor_tensor(qr, cre, lre, ALU.mult)
                order.done(nc.gpsimd.tensor_tensor(t, cim, lim, ALU.mult))
                order.done(nc.gpsimd.tensor_tensor(qr, qr, t, ALU.subtract))
                low(3 + 3 * i)
                nc.gpsimd.tensor_tensor(qi, cim, lre, ALU.mult)
                order.done(nc.gpsimd.tensor_tensor(t, cre, lim, ALU.mult))
                order.done(nc.gpsimd.tensor_tensor(qi, qi, t, ALU.add))
                low(4 + 3 * i)
                nc.gpsimd.tensor_scalar(qi, qi, -1.0, 0.0, ALU.mult, ALU.add).then_inc(q_built, 1)
                low(5 + 3 * i)
            for n in range(15, 18):
                low(n)

            def mask(h):
                diag = sp[:, h % 2, :].rearrange("p (b c) -> p b c", c=640)[:, :, 0:P]
                nc.gpsimd.affine_select(out=diag, in_=diag, compare_op=ALU.is_gt, fill=0.0, base=0,
                                        pattern=[[0, 3], [1, P]], channel_multiplier=-1)
                last = sp[:, h % 2, 512:512 + P]
                return nc.gpsimd.affine_select(out=last, in_=last, compare_op=ALU.is_gt, fill=0.0, base=0,
                                               pattern=[[1, P]], channel_multiplier=-1)

            for h in range(HEADS + 1):
                if h < HEADS:
                    pool.wait_ge(soft_done, h + 1)
                    mask(h).then_inc(soft_masked, 1)
                if h >= 1:
                    pool.wait_ge(a_exp, h)
                    mask(h - 1).then_inc(a_masked, 1)
            with pool.Fori(0, (N_END - N_MK) // 4) as i:
                for s in range(4):
                    low(N_MK + s, i)

        @block.tensor
        def _(pe):
            def three(parts, first, last):
                for out, s_hi, s_lo, m_hi_, m_lo_ in parts:
                    pe.matmul(out, s_hi, m_hi_, start=first, stop=False)
                    pe.matmul(out, s_hi, m_lo_, start=False, stop=False)
                    ins = pe.matmul(out, s_lo, m_hi_, start=False, stop=last)
                return ins

            def wide_three(out, stationary, moving, first, last):
                pe.matmul(out, stationary[0], moving[0], start=first, stop=False, skip_group_check=True)
                pe.matmul(out, stationary[0], moving[1], start=False, stop=False, skip_group_check=True)
                return pe.matmul(out, stationary[1], moving[0], start=False, stop=last, skip_group_check=True)

            def weight(n, kt, width=P):
                return (w_hi[:, n % 2, kt * width:(kt + 1) * width], w_lo[:, n % 2, kt * width:(kt + 1) * width])

            def ready(n, e, i=0):
                pe.wait_ge(lo_done, n + 1 + i * 4)
                if e >= 2:
                    pe.wait_ge(evacuated, e - 1 + i * 4)

            def project(n, e, i=0, split_from=None):
                ready(n, e, i)
                for kt in range(KT):
                    if split_from is not None:
                        pe.wait_ge(h_split, split_from + kt + 1)
                    hi, lo = weight(n, kt)
                    ins = three([(slot(e)[:, a, :], hi, lo, halves(h_hi[:, kt, :])[:, a, :],
                                  halves(h_lo[:, kt, :])[:, a, :]) for a in range(2)], kt == 0, kt == KT - 1)
                ins.then_inc(block_done, 1)

            def feature_sums(bank, widths):
                at_ = 0
                for b, w in enumerate(widths):
                    ins = pe.matmul(aux[:, bank + b, 0:w], ones, acc[:, at_:at_ + w], start=True, stop=True)
                    at_ += w
                return ins

            project(0, 0, split_from=0)
            pe.wait_ge(consts_loaded, 16)
            pe.wait_ge(acc_added, 8)
            feature_sums(0, (HALF, HALF))
            for i in range(4):
                pe.matmul(aux[:, 2, i:i + 1], acc[:, P * i:P * (i + 1)], ones[:, 0:1], start=True, stop=True)
            ins = pe.matmul(aux[0:NS, 2, 4:5], acc[:, TP:T], ones[:, 0:1], start=True, stop=True)
            ins.then_inc(stats_done, 1)
            for n in range(1, 4):
                project(n, n)

            pe.wait_ge(wt_built, 1)
            pe.wait_ge(root_done, 1)
            for g in range(8):
                b, wt = g // 2, (wtre, wtim)[g % 2]
                if g >= 4:
                    pe.wait_ge(w2_copied, g - 3)
                for r in range(4):
                    ins = pe.transpose(aux[:, g % 4, P * r:P * (r + 1)],
                                       wt[:, 4 * b + r].rearrange("p j g -> p (j g)"), ident)
                ins.then_inc(wt_turned, 1)
            pe.wait_ge(w2_copied, 5)
            pe.wait_ge(negc_done, 1)
            for k in range(PAIRS):
                out = aux[:, 0, GP * k:GP * (k + 1)]
                pe.matmul(out, wtre[:, k].rearrange("p j g -> p (j g)"), cmat[:, 0, k, :], start=True, stop=False)
                ins = pe.matmul(out, wtim[:, k].rearrange("p j g -> p (j g)"), ncim[:, k, :], start=False, stop=True)
            ins.then_inc(kernel_done, 1)

            def chunk_states(b):
                if b == 0:
                    pe.wait_ge(w2_copied, 8)
                    pe.wait_ge(u2_act, 1)
                    pe.wait_ge(u2_dve, 1)
                    pe.wait_ge(mt_built, 1)
                if b >= 2:
                    pe.wait_ge(v_read, b - 1)
                for part, w2 in enumerate((w2re, w2im)):
                    for r in range(4):
                        k = 4 * b + r
                        ins = pe.matmul(aux[:, 2 * (b % 2) + part, P * r:P * (r + 1)], w2[:, k, :], u2[:, k, :],
                                        start=True, stop=True)
                ins.then_inc(v_done, 1)

            for n in range(N_Q, N_V):
                project(n, n)
                if n % 2 == 1:
                    chunk_states((n - N_Q) // 2)
            pe.wait_ge(v_read, 3)
            for part, w2 in enumerate((w2re, w2im)):
                for k in range(PAIRS):
                    ins = pe.matmul(aux[:, 0, P * part + NS * k:P * part + NS * (k + 1)], w2[:, k, :],
                                    u_last[:, k, :], start=True, stop=True)
            ins.then_inc(vs_done, 1)

            for n in range(N_V, N_GLU):
                pair, part = divmod(n - N_V, 2)
                ready(n, N_V + pair)
                for tt in range(4):
                    bank = 2 * (pair % 2) + tt // 2
                    for j in range(4):
                        kt = 4 * part + j
                        hi, lo = weight(n, j, 2 * P)
                        h = (h_hi[:, kt, P * tt:P * (tt + 1)], h_lo[:, kt, P * tt:P * (tt + 1)])
                        wide_three(pj[:, bank, 2 * P * (tt % 2):2 * P * (tt % 2 + 1)], h, (hi, lo),
                                   kt == 0 and tt % 2 == 0, kt == KT - 1)
                for j in range(4):
                    kt = 4 * part + j
                    ins = wide_three(aux[0:NS, 1, 2 * P * pair:2 * P * (pair + 1)],
                                     (h_hi[:, kt, TP:T], h_lo[:, kt, TP:T]), weight(n, j, 2 * P),
                                     kt == 0 and pair == 0, kt == KT - 1)
                ins.then_inc(block_done, 1)

            pe.wait_ge(states_done, 4)
            pe.wait_ge(q_built, CH)
            pe.wait_ge(v_read, 4)
            pe.wait_ge(vs_read, 1)
            pe.wait_ge(vtail_read, 1)
            for a in range(4):
                for r in range(4):
                    k = 4 * a + r
                    out = aux[:, a, P * r:P * (r + 1)]
                    pe.matmul(out, qre[:, k].rearrange("p i g -> p (i g)"), sre3[:, k, 0:NCH], start=True, stop=False)
                    pe.matmul(out, qim[:, k].rearrange("p i g -> p (i g)"), sim3[:, k, 0:NCH], start=False, stop=False)
                    ins = pe.matmul(out, mt[:, k, :], u2[:, k, :], start=False, stop=True)
                ins.then_inc(y_done, 1)
            pe.wait_ge(evacuated, N_V + 2)
            for k in range(PAIRS):
                out = pj[0:GP, 0, NS * k:NS * (k + 1)]
                pe.matmul(out, qre[:, k, 0, :], h0(0, k), start=True, stop=False)
                pe.matmul(out, qim[:, k, 0, :], h0(1, k), start=False, stop=False)
                ins = pe.matmul(out, mt[:, k, 0:GP], u_first[:, k, :], start=False, stop=True)
            ins.then_inc(y_done, 1)

            def scores(h):
                pair, r0 = h // 2, DH * (h % 2)
                if h == 0:
                    pe.wait_ge(gelu_done, 1)
                    pe.wait_ge(evacuated, 16)
                if h >= 2:
                    pe.wait_ge(a_exp, h - 1)
                for i in range(4):
                    if i == 3 and h >= 1:
                        for n in range(PAGES * (h - 1), PAGES * h):
                            decode_scores(n)
                    ins = pe.matmul(at(h, i, P * i), kT[r0:r0 + DH, pair, P * i:P * (i + 1)],
                                    qT[r0:r0 + DH, pair, P * i:TP], start=(i < 3), stop=(i == 3),
                                    skip_group_check=True)
                ins.then_inc(qk_done, 1)

            def cumulate(h):
                pe.wait_ge(soft_masked, h + 1)
                for i in range(4):
                    for j in range(i, 4):
                        ins = pe.matmul(at(h, i, P * j), ntri if i == j else nones, sp_at(h, j, P * j),
                                        start=False, stop=(j == 3), skip_group_check=True)
                ins.then_inc(cum_done, 1)

            def values(h):
                pair, r0 = h // 2, DH * (h % 2)
                pe.wait_ge(a_masked, h + 1)
                if h % 2 == 0 and pair >= 2:
                    pe.wait_ge(o_read, pair - 1)
                for i in range(4):
                    ins = pe.matmul(o_bank(pair)[r0:r0 + DH, P * i:TP], vtok[:, i, DH * h:DH * (h + 1)],
                                    sp_at(h, i, P * i), start=(i == 0), stop=(i == 3), skip_group_check=True)
                ins.then_inc(av_done, 1)

            def dcol(t, b, pair):
                at_ = (t * NS + b) * HEADS + 2 * pair
                return slice(at_, at_ + 2)

            def decode_scores(n):
                b, t = n // PAGES, n % PAGES
                tensor = pj if b % 2 == 0 else aux
                pe.wait_ge(kpg_loaded[n % 4], 16 * (n // 4 + 1))
                for pair in range(AT):
                    ins = pe.matmul(tensor[:, 2, dcol(t, b, pair)], kpg[:, n % 4, P * pair:P * (pair + 1)],
                                    qbd[:, pair, b, :], start=False, stop=True, skip_group_check=True)
                ins.then_inc(dscore_pg, 1)

            pe.wait_ge(qbd_ready, 1)
            scores(0)
            for h in range(HEADS + 1):
                if h >= 1:
                    values(h - 1)
                if h + 1 < HEADS:
                    scores(h + 1)
                if h < HEADS:
                    cumulate(h)
                if h == HEADS - 1:
                    pe.wait_ge(a_exp, HEADS - 1)
                    for n in range(PAGES * (NS - 1), PAGES * NS):
                        decode_scores(n)

            pe.wait_ge(acc_added, 12)
            pe.wait_ge(dz_ready, 1)
            pe.matmul(aux[:, 2, 0:MT], ones, acc[:, 0:MT], start=True, stop=False)
            pe.matmul(aux[:, 2, 0:MT], ones, acc[:, MT:2 * MT], start=False, stop=True).then_inc(stats_done, 1)

            for g in range(2):
                pe.wait_ge(lo_done, N_GLU + g + 1)
                for j in range(2):
                    e = N_GLU + 2 * g + j
                    pe.wait_ge(evacuated, e - 1)
                    if e == N_GLU:
                        pe.wait_ge(y_split, AT)
                        pe.wait_ge(a_exp, HEADS)
                    if e == N_GLU + 1:
                        pe.wait_ge(o_read, 4)
                    for kt in range(AT):
                        hi, lo = (w[:, j * P:(j + 1) * P] for w in weight(N_GLU + g, kt, 2 * P))
                        ins = three([(slot(e)[:, a, :], hi, lo, halves(h_hi[:, AT + kt, :])[:, a, :],
                                      halves(h_lo[:, AT + kt, :])[:, a, :]) for a in range(2)],
                                    kt == 0, kt == AT - 1)
                ins.then_inc(block_done, 1)

            pe.wait_ge(dsp_ready, 1)
            W = NS * HEADS
            pe.matmul(aux[:, 0, P:P + W], ntri, dz[:, 1, 0:W], start=True, stop=False)
            pe.matmul(aux[:, 0, P:P + W], nones, dz[:, 1, W:2 * W], start=False, stop=True)
            pe.matmul(aux[:, 0, P + W:P + 2 * W], ntri, dz[:, 1, W:2 * W], start=True, stop=True).then_inc(
                dcum_done, 1)
            pe.wait_ge(da_ready, 1)
            for n in range(NS * PAGES):
                b, t = n // PAGES, n % PAGES
                pe.wait_ge(vpg_loaded[n % 4], 16 * (n // 4 + 1))
                for pair in range(AT):
                    ins = pe.matmul(aux[:, 1, P * t + (b * AT + pair) * 2:P * t + (b * AT + pair) * 2 + 2],
                                    vpg[:, n % 4, P * pair:P * (pair + 1)], dz[:, 3, dcol(t, b, pair)],
                                    start=True, stop=True)
                ins.then_inc(dav_pg, 1)

            pe.wait_ge(acc_added, 16)
            pe.wait_ge(root_done, 2)
            feature_sums(2, (HALF, HALF)).then_inc(stats_done, 1)

            pe.wait_ge(m_split, KT)
            with pe.Fori(0, 2) as i:
                for s in range(4):
                    n, e = N_MK + s, N_MK + 2 + s
                    ready(n, e, i)
                    for kt in range(KT):
                        hi, lo = weight(n, kt)
                        ins = three([(slot(e)[:, 0, 0:MT], hi, lo, m_hi[:, kt, :], m_lo[:, kt, :])],
                                    kt == 0, kt == KT - 1)
                    ins.then_inc(block_done, 1)
            pe.wait_ge(acc_added, 20)
            pe.wait_ge(dav_read, 1)
            feature_sums(0, (HALF, HALF)).then_inc(stats_done, 1)
            with pe.Fori(0, 2) as i:
                for s in range(4):
                    n = N_MV + s
                    pe.wait_ge(lo_done, n + 1 + i * 4)
                    if s % 2 == 0:
                        pe.wait_ge(evacuated, i * 4 + (N_MV + 2) if s == 2 else i * 3 + (N_MV + 1))
                    pair, part = divmod(s, 2)
                    for tt in range(2):
                        for j in range(4):
                            kt = 4 * part + j
                            m = (m_hi[:, kt, P * tt:P * (tt + 1)], m_lo[:, kt, P * tt:P * (tt + 1)])
                            ins = wide_three(pj[:, 2 * pair, 2 * P * tt:2 * P * (tt + 1)], m,
                                             weight(n, j, 2 * P), kt == 0 and tt == 0, kt == KT - 1)
                    ins.then_inc(block_done, 1)

            pe.wait_ge(h_split, 16)
            with pe.Fori(0, 2) as i:
                for s in range(4):
                    project(N_OUT + s, N_OUT + 2 + s, i)
            pe.wait_ge(acc_added, 28)
            pe.wait_ge(root_done, 4)
            feature_sums(0, (HALF, HALF)).then_inc(stats_done, 1)
            with pe.Fori(0, 2) as i:
                for s in range(4):
                    project(N_MQ + s, N_MQ + 2 + s, i, split_from=16 if s == 0 else None)

            def mem_scores(h):
                if h == 0:
                    pe.wait_ge(evacuated, N_MO + 2)
                    pe.wait_ge(root_done, 5)
                if h >= 2:
                    pe.wait_ge(p_exp, 4 * (h - 1))
                for qt in range(4):
                    for dd in range(2):
                        ins = pe.matmul(aux[:, 2 * (h % 2) + qt // 2, MT * (qt % 2):MT * (qt % 2 + 1)],
                                        qm[:, 2 * h + dd, P * qt:P * (qt + 1)], mkT[:, 2 * h + dd, :],
                                        start=(dd == 0), stop=(dd == 1))
                ins.then_inc(s_done, 1)

            def window(f, row):
                at_ = ROWS * (row // MH) + ROWS - 1 - row
                return qz[f // 4][:, f % 4, at_:at_ + ROWS]

            def decode_values(b):
                pe.wait_ge(vmd_loaded[b % 2], 16 * (b // 2 + 1))
                for h in range(MH):
                    row = MH * b + h
                    for t in range(2):
                        flat = pz[:, t].rearrange("p c w -> p (c w)")
                        at_ = ROWS * row + ROWS - 1 - row
                        ins = pe.matmul(pj[0:ROWS, 1, 0:MT], flat[:, at_:at_ + ROWS],
                                        vmd[:, b % 2, D * t + MT * h:D * t + MT * (h + 1)],
                                        start=(row == 0 and t == 0), stop=(row == ROWS - 1 and t == 1),
                                        skip_group_check=True)
                ins.then_inc(vmd_used, 1)

            mem_scores(0)
            mem_scores(1)
            pe.wait_ge(qz_ready, 1)
            for b in range(NS):
                pe.wait_ge(kmd_loaded[b % 3], 16 * (b // 3 + 1))
                for f in range(KT):
                    ins = pe.matmul(pj[0:ROWS, 3, 0:MT], window(f, MH * b + f // 2),
                                    kmd[:, b % 3, MT * f:MT * (f + 1)],
                                    start=(b == 0 and f == 0), stop=(b == NS - 1 and f == KT - 1),
                                    skip_group_check=True)
                ins.then_inc(kmd_used, 1)
            for h in range(MH):
                pe.wait_ge(p_ready, h + 1)
                for kt in range(2):
                    if h + kt > 0:
                        pe.wait_ge(pt_copied, 2 * h + kt)
                    for qt in range(4):
                        ins = pe.transpose(pj[:, 0, P * qt:P * (qt + 1)],
                                           prob[:, h % 2, qt, P * kt:P * (kt + 1)], ident)
                    ins.then_inc(pt_done, 1)
                    if h + kt == 0:
                        pe.wait_ge(drow_ready, 1)
                        for t in range(2):
                            ins = pe.transpose(pj[:, 2, ROWS * t:ROWS * (t + 1)], drow[:, P * t:P * (t + 1)],
                                               ident[0:ROWS, 0:ROWS])
                        ins.then_inc(dp_turned, 1)
                        pe.wait_ge(dp_copied, 1)
                    decode_values(2 * h + kt)
                if h + 2 < MH:
                    mem_scores(h + 2)
                pe.wait_ge(pt_copied, 2 * h + 2)
                if h >= 1:
                    pe.wait_ge(o_lo, h)
                for dd in range(2):
                    for kt in range(2):
                        c = MT * h + P * dd
                        ins = pe.matmul(pj[:, 2 + dd, :], mv[:, kt, c:c + P], probT[:, kt, :],
                                        start=(kt == 0), stop=(kt == 1))
                ins.then_inc(o_done, 1)
            pe.wait_ge(do_rows, 1)
            for dd in range(2):
                ins = pe.transpose(pj[:, 0, ROWS * dd:ROWS * (dd + 1)], drow[:, P * dd:P * (dd + 1)],
                                   ident[0:ROWS, 0:ROWS])
            ins.then_inc(do_turned, 1)

            pe.wait_ge(o_lo, MH)
            pe.wait_ge(do_lo, 1)
            with pe.Fori(0, 2) as i:
                for s in range(4):
                    project(N_MO + s, N_MO + 2 + s, i)

            pe.wait_ge(acc_added, 36)
            feature_sums(0, (HALF, HALF)).then_inc(stats_done, 1)

            with pe.Fori(0, (N_DOWN - N_GU) // 4) as i:
                for s in range(4):
                    project(N_GU + s, N_GU + 2 + s, i, split_from=24 if s == 0 else None)
            with pe.Fori(0, 2) as i:
                for m in range(4):
                    e = N_DOWN + 2 + m
                    pe.wait_ge(evacuated, e - 1 + i * 4)
                    for c, width in enumerate(DOWN_CHUNKS):
                        n = N_DOWN + 3 * m + c
                        pe.wait_ge(lo_done, n + 1 + i * 12)
                        for j in range(width):
                            kt = sum(DOWN_CHUNKS[:c]) + j
                            if m == 0:
                                pe.wait_ge(a_split, kt + 1)
                            hi, lo = weight(n, j)
                            ins = three([(slot(e)[:, a, :], hi, lo, halves(a_hi[:, kt, :])[:, a, :],
                                          halves(a_lo[:, kt, :])[:, a, :]) for a in range(2)],
                                        kt == 0, kt == FT - 1)
                        ins.then_inc(block_done, 1)
            pe.wait_ge(acc_added, 44)
            feature_sums(0, (HALF, HALF)).then_inc(stats_done, 1)

        @block.scalar
        def _(act):
            order = Order(act, act_order)

            def high(n, i=0, step=4):
                act.wait_ge(raw_loaded[n % 4], raw_count(n, i, step))
                if n >= 2:
                    act.wait_ge(block_done, n - 1 + i * step)
                nc.scalar.activation(w_hi[:, n % 2, :], w_raw[:, n % 4, :], ACT.Copy).then_inc(hi_done, 1)

            def square(src, width, j, i=0, per=0):
                if not (isinstance(j, int) and j == 0):
                    act.wait_ge(acc_added, j + i * per)
                nc.scalar.activation(sq[:, 0:width], src, ACT.Square).then_inc(sq_ready, 1)

            def root(group, out, src, features):
                act.wait_ge(stats_done, group + 1)
                nc.scalar.activation(out, src, ACT.Sqrt, scale=1.0 / features, bias=eps_col).then_inc(root_done, 1)

            def split_high(kt, gain):
                nc.scalar.activation(h_hi[:, kt, :], x[:, kt, :], ACT.Copy, scale=col(gain, kt)).then_inc(
                    h_hi_done, 1)

            eps_col = EPS
            sums01 = aux[:, 0:2, 0:HALF]
            sums23 = aux[:, 2:4, 0:HALF]

            act.wait_ge(cols_loaded, 16)
            nc.scalar.activation(sm[:, 8, :], col("log_dt", 0, PAIRS), ACT.Exp).then_inc(dt_done, 1)
            act.wait_ge(angle_done, 1)
            nc.scalar.activation(sm[:, 11, :], sm[:, 9, :], ACT.Exp)
            nc.scalar.activation(sm[:, 14:16, :], sm[:, 12:14, :], ACT.Sin).then_inc(polar_done, 1)
            for kt in range(KT):
                act.wait_ge(x_loaded[kt // 2], 16)
                split_high(kt, "g_mix")
                square(x[:, kt, :], T, kt)
                if kt < 2:
                    high(kt)
            act.wait_ge(s5_loaded, 48)
            nc.scalar.activation(ncim, cmat[:, 1], ACT.Copy, scale=-1.0).then_inc(negc_done, 1)
            high(2)
            act.wait_ge(stats_done, 1)
            nc.scalar.activation(rinv_col[:, 0:4], aux[:, 2, 0:4], ACT.Sqrt, scale=1.0 / D, bias=eps_col)
            nc.scalar.activation(rinv_col[0:NS, 4:5], aux[0:NS, 2, 4:5], ACT.Sqrt, scale=1.0 / D, bias=eps_col)
            root(0, halves(rinv[:, :]), sums01, D)
            for n in range(3, 6):
                high(n)
            for g in range(8):
                act.wait_ge(wt_turned, g + 1)
                w2 = (w2re, w2im)[g % 2]
                nc.scalar.activation(w2[:, 4 * (g // 2):4 * (g // 2) + 4, :].rearrange("p k s -> p (k s)"),
                                     aux[:, g % 4, :], ACT.Copy).then_inc(w2_copied, 1)

            act.wait_ge(evacuated, 4)
            act.wait_ge(u_zeroed, 1)
            for q in range(4):
                rows = slice(GP * q, GP * (q + 1))
                for j in range(2):
                    ins = nc.scalar.activation(
                        u2[GP * j:GP * (j + 1), :, :].rearrange("p (a q) c -> p a q c", q=4)[:, :, q, :],
                        uT[rows, :, 0:TP].rearrange("p a (c j) -> p a c j", j=CH)[:, :, :, j], ACT.Copy)
                ins = nc.scalar.activation(
                    u_first[0:GP, :, :].rearrange("p (a q) b -> p a q b", q=4)[:, :, q, :],
                    uT[rows, :, TP:T], ACT.Copy)
            ins.then_inc(u2_act, 1)

            act.wait_ge(kernel_done, 1)
            act.wait_ge(k0_added, 1)
            act.wait_ge(mt_zeroed, 1)
            mt4 = mt[:, :, :].rearrange("p k (i g) -> p k i g", i=CH)
            for lag in range(CH):
                r = GP * (CH - 1 - lag)
                src = (dskip[r:r + GP] if lag == 0 else
                       aux[r:r + GP, 0, :].rearrange("p (k g) -> p k g", k=PAIRS))
                for j in range(CH - lag):
                    ins = nc.scalar.activation(mt4[GP * j:GP * (j + 1), :, j + lag, :], src, ACT.Copy)
            ins.then_inc(mt_built, 1)

            for n in range(6, 18):
                high(n)

            act.wait_ge(y_done, 5)
            act.wait_ge(ssm_out_done, 2)
            yT4 = yT[:, :, 0:TP].rearrange("p a (c i) -> p a c i", i=CH)
            for q in range(4):
                rows = slice(GP * q, GP * (q + 1))
                for i in range(CH):
                    nc.scalar.activation(yT4[rows, :, :, i], aux[GP * i:GP * (i + 1), :, P * q:P * (q + 1)],
                                         ACT.Gelu_apprx_tanh)
                ins = nc.scalar.activation(
                    yT[rows, :, TP:T], pj[0:GP, 0, 0:PAIRS * NS].rearrange("p (a q b) -> p a q b", a=4, q=4)[:, :, q],
                    ACT.Gelu_apprx_tanh)
            ins.then_inc(gelu_done, 1)
            act.wait_ge(gelu_done, 1)
            act.wait_ge(block_done, N_GLU)
            for a in range(AT):
                nc.scalar.activation(h_hi[:, AT + a, :], yT[:, a, :], ACT.Copy).then_inc(y_hi_done, 1)

            def soft(h):
                act.wait_ge(capped, h + 1)
                for _, run in spans(h):
                    ins = nc.scalar.activation(run, run, ACT.Exp, bias=col("sb_bias", h))
                order.done(ins)
                for _, run in spans(h):
                    ins = nc.scalar.activation(run, run, ACT.Ln, bias=1.0)
                ins.then_inc(soft_log, 1)

            soft(0)
            for h in range(HEADS):
                if 2 <= h < 6:
                    g = h - 2
                    act.wait_ge(mem_loaded, 16)
                    square(memx[:, 2 * g:2 * g + 2, :].rearrange("p a t -> p (a t)"), 2 * MT, 8 + g)
                if h + 1 < HEADS:
                    soft(h + 1)
                act.wait_ge(cum_done, h + 1)
                for src, run in spans(h):
                    ins = nc.scalar.activation(run, src, ACT.Exp, bias=col("sb_bias", h))
                ins.then_inc(a_exp, 1)

            act.wait_ge(dz_ready, 1)
            order.done(nc.scalar.activation(dz[:, 1, :], dz[:, 1, :], ACT.Exp))
            nc.scalar.activation(dz[:, 1, :], dz[:, 1, :], ACT.Ln, bias=1.0).then_inc(dsoft_log, 1)
            root(1, rinv_m[:, :], aux[:, 2, 0:MT], D)
            for m in range(AT):
                act.wait_ge(block_done, N_GLU + m // 2 + 1)
                nc.scalar.activation(slot(m), slot(m), ACT.Sigmoid, bias=col("b_glu", m)).then_inc(sig_done, 1)
                if m % 2 == 1:
                    high(N_MK + m // 2)
            for kt in range(KT):
                act.wait_ge(m_scaled, kt + 1)
                nc.scalar.activation(m_hi[:, kt, :], memx[:, kt, :], ACT.Copy).then_inc(m_hi_done, 1)
            act.wait_ge(da_arg, 1)
            nc.scalar.activation(dz[:, 3, :], dz[:, 2, :], ACT.Exp).then_inc(da_ready, 1)
            act.wait_ge(evacuated, N_GLU + AT)
            for a in range(AT):
                square(yT[:, a, :], T, 12 + a)
            root(2, halves(rinv[:, :]), sums23, SBW)
            act.wait_ge(dav_read, 1)
            for a in range(AT):
                square(osb[:, a, :], T, 16 + a)
            for n in range(N_MK + 2, N_MV + 2):
                high(n)
            act.wait_ge(mix_scaled, AT)
            root(3, halves(rinv[:, :]), sums01, SBW)
            act.wait_ge(block_done, N_MK)
            for s in range(8):
                kt = (AT + s) % KT
                act.wait_ge(mix_scaled, s + 1)
                src = yT if kt >= AT else osb
                nc.scalar.activation(h_hi[:, kt, :], src[:, kt % AT, :], ACT.Copy).then_inc(h_hi_done, 1)
                high(N_MV + 2 + s)

            def residual(base, j0):
                with act.Fori(0, 2) as i:
                    for s in range(4):
                        high(base + 2 + s, i)
                        act.wait_ge(evacuated, base + 3 + s + i * 4)
                        square(x[:, i * 4 + s, :], T, j0 + s, i, 4)

            def next_norm(group, gain, free):
                act.wait_ge(block_done, free)
                for kt in range(KT):
                    split_high(kt, gain)
                    if kt == 1:
                        root(group, halves(rinv[:, :]), sums01, D)

            residual(N_OUT, 20)
            next_norm(4, "g_mem_q", N_MQ)
            with act.Fori(0, 2) as i:
                for s in range(4):
                    high(N_MQ + 2 + s, i)

            def mem_exp(h):
                act.wait_ge(smax_done, h + 1)
                if h >= 2:
                    act.wait_ge(pt_done, 2 * (h - 1))
                for qt in range(4):
                    nc.scalar.activation(prob[:, h % 2, qt, :],
                                         aux[:, 2 * (h % 2) + qt // 2, MT * (qt % 2):MT * (qt % 2 + 1)], ACT.Exp,
                                         bias=stat[:, h % 2, 0, qt:qt + 1],
                                         accum_out=stat[:, h % 2, 1, qt:qt + 1]).then_inc(p_exp, 1)

            mem_exp(0)
            mem_exp(1)
            act.wait_ge(drow_max, 1)
            nc.scalar.activation(drow[:, :], pj[0:ROWS, 3, 0:MT], ACT.Exp, bias=dstat[:, 0:1],
                                 accum_out=dstat[:, 1:2]).then_inc(drow_exp, 1)
            for h in range(MH):
                for kt in range(2):
                    act.wait_ge(pt_done, 2 * h + kt + 1)
                    nc.scalar.activation(probT[:, kt, :], pj[:, 0, :], ACT.Copy).then_inc(pt_copied, 1)
                    if h + kt == 0:
                        act.wait_ge(dp_turned, 1)
                        act.wait_ge(z_cleared, 1)
                        nc.scalar.activation(pz[:, :, :, ROWS - 1], pj[:, 2, 0:2 * ROWS].rearrange(
                            "p (t c) -> p t c", t=2), ACT.Copy).then_inc(dp_copied, 1)
                if h + 2 < MH:
                    mem_exp(h + 2)
                if h == MH - 1:
                    act.wait_ge(vmd_used, NS)
                    nc.scalar.activation(drow[:, :], pj[0:ROWS, 1, 0:MT], ACT.Copy).then_inc(do_rows, 1)
                act.wait_ge(o_done, h + 1)
                nc.scalar.activation(h_hi[:, 2 * h:2 * h + 2, 0:TP], pj[:, 2:4, :], ACT.Copy).then_inc(o_hi, 1)
            act.wait_ge(do_turned, 1)
            do_tiles = pj[:, 0, 0:2 * ROWS].rearrange("p (d b h) -> p h d b", d=2, h=MH)
            nc.scalar.activation(h_hi[:, :, TP:T].rearrange("p (h d) b -> p h d b", d=2), do_tiles,
                                 ACT.Copy).then_inc(do_hi, 1)

            residual(N_MO, 28)
            next_norm(5, "g_ffn", N_GU)

            with act.Fori(0, FT // 2) as i:
                for c in range(2):
                    n = N_GU + 2 * c
                    act.wait_ge(evacuated, n + 3 + i * 4)
                    nc.scalar.activation(gate_keep[:, i * 2 + c, :], gate[:, c, TP:T + 2], ACT.Copy)
                    act.wait_ge(a_split, c + i * 2)
                    nc.scalar.activation(conv[:, c, :], gate[:, c, 2:T + 2], ACT.Identity,
                                         scale=cols[:, bass.ds(i * 2 + (COL["conv_w2"] + c), 1)],
                                         bias=cols[:, bass.ds(i * 2 + (COL["conv_b"] + c), 1)]
                                         ).then_inc(tap2_done, 1)
                    high(n + 2, i)
                    act.wait_ge(conv_done, c + 1 + i * 2)
                    nc.scalar.activation(conv[:, c, :], conv[:, c, :], ACT.Gelu_apprx_tanh).then_inc(ff_gelu, 1)
                    high(n + 3, i)
                    act.wait_ge(evacuated, n + 4 + i * 4)
                    nc.scalar.activation(a_hi[:, i * 2 + c, :], conv[:, c, :], ACT.Copy).then_inc(a_hi_done, 1)
            for m in range(KT):
                for c in range(3):
                    n = N_DOWN + 3 * m + c + 2
                    if n < N_END:
                        high(n)
                act.wait_ge(evacuated, N_DOWN + 3 + m)
                square(x[:, m, :], T, 36 + m)
            root(6, halves(rinv[:, :]), sums01, D)

        @block.vector
        def _(dve):
            order = Order(dve, dve_order)
            tt, ts, stt = nc.vector.tensor_tensor, nc.vector.tensor_scalar, nc.vector.scalar_tensor_tensor

            def add_square(j, first, width=T, group=0, i=0, per=0):
                dve.wait_ge(sq_ready, j + 1 + i * per)
                if first:
                    if group:
                        dve.wait_ge(stats_done, group)
                    nc.vector.tensor_copy(acc[:, 0:width], sq[:, 0:width]).then_inc(acc_added, 1)
                else:
                    dve.wait_ge(acc_added, j + i * per)
                    tt(acc[:, 0:width], acc[:, 0:width], sq[:, 0:width], ALU.add).then_inc(acc_added, 1)

            def split_low(kt, gain, at_):
                dve.wait_ge(h_hi_done, at_)
                stt(out=h_lo[:, kt, :], in0=x[:, kt, :], scalar=col(gain, kt), in1=h_hi[:, kt, :].bitcast(F32),
                    op0=ALU.mult, op1=ALU.subtract).then_inc(h_split, 1)

            def invert(group, out=None):
                dve.wait_ge(root_done, group + 1)
                out = rinv[:, :] if out is None else out
                nc.vector.reciprocal(out, out).then_inc(rinv_done, 1)
                dve.wait_ge(rinv_done, group + 1)

            def v(i):
                return sm[:, i, :]

            def cmul(out_re, out_im, a_re, a_im, b_re, b_im, t, signal=None):
                tt(t[0], a_re, b_re, ALU.mult)
                tt(t[1], a_im, b_im, ALU.mult)
                tt(t[2], a_re, b_im, ALU.mult)
                order.done(tt(t[3], a_im, b_re, ALU.mult))
                tt(out_re, t[0], t[1], ALU.subtract)
                ins = tt(out_im, t[2], t[3], ALU.add)
                if signal is None:
                    order.done(ins)
                else:
                    ins.then_inc(signal, 1)
                    dve.wait_ge(signal, 1)

            small = [v(i) for i in range(25, 29)]
            dve.wait_ge(cols_loaded, 16)
            lam_re, lam_im = col("lam_re", 0, PAIRS), col("lam_im", 0, PAIRS)
            dve.wait_ge(dt_done, 1)
            tt(v(9), lam_re, v(8), ALU.mult)
            order.done(tt(v(10), lam_im, v(8), ALU.mult))
            for out, turn in ((12, 0.25), (13, 0.0)):
                order.done(ts(v(25), v(10), TWO_PI_INV, turn, ALU.mult, ALU.add))
                order.done(ts(v(25), v(25), ROUND, None, ALU.add))
                order.done(ts(v(25), v(25), ROUND, None, ALU.subtract))
                order.done(stt(out=v(26), in0=v(25), scalar=-TWO_PI_A, in1=v(10), op0=ALU.mult, op1=ALU.add))
                order.done(stt(out=v(26), in0=v(25), scalar=-TWO_PI_B, in1=v(26), op0=ALU.mult, op1=ALU.add))
                order.done(stt(out=v(26), in0=v(25), scalar=-TWO_PI_C, in1=v(26), op0=ALU.mult, op1=ALU.add))
                order.done(ts(v(26), v(26), HALF_PI if turn else 0.0, PI_IN, ALU.add, ALU.min))
                ins = ts(v(out), v(26), -PI_IN, None, ALU.max)
                if out == 12:
                    order.done(ins)
            ins.then_inc(angle_done, 1)

            for kt in range(KT):
                split_low(kt, "g_mix", kt + 1)
                add_square(kt, kt == 0)

            dve.wait_ge(polar_done, 1)
            tt(v(0), v(11), v(14), ALU.mult)
            tt(v(1), v(11), v(15), ALU.mult)
            tt(v(22), v(11), v(11), ALU.mult)
            order.done(tt(v(24), lam_re, lam_re, ALU.mult))
            order.done(tt(v(23), v(22), v(22), ALU.mult))
            cmul(v(18), v(19), v(14), v(15), v(14), v(15), small)
            cmul(v(20), v(21), v(18), v(19), v(18), v(19), small)
            cmul(v(2), v(3), v(0), v(1), v(0), v(1), small)
            cmul(v(4), v(5), v(2), v(3), v(0), v(1), small)
            tt(v(6), v(23), v(20), ALU.mult)
            tt(v(7), v(23), v(21), ALU.mult).then_inc(powers_done, 1)
            order.done(tt(v(29), lam_im, lam_im, ALU.mult))
            tt(v(24), v(24), v(29), ALU.add)
            order.done(ts(v(30), v(0), -1.0, None, ALU.add))
            nc.vector.reciprocal(v(24), v(24))
            tt(v(25), v(30), lam_re, ALU.mult)
            tt(v(26), v(1), lam_im, ALU.mult)
            tt(v(27), v(1), lam_re, ALU.mult)
            order.done(tt(v(28), v(30), lam_im, ALU.mult))
            tt(v(25), v(25), v(26), ALU.add)
            order.done(tt(v(27), v(27), v(28), ALU.subtract))
            tt(v(16), v(25), v(24), ALU.mult)
            order.done(tt(v(17), v(27), v(24), ALU.mult))

            def wide(i):
                return v(i).unsqueeze(2).broadcast_to([P, PAIRS, GP])

            t4 = [tmp[:, i, :].rearrange("p (k g) -> p k g", k=PAIRS) for i in range(4)]
            dve.wait_ge(s5_loaded, 48)
            cmul(wtre[:, :, 3, :], wtim[:, :, 3, :], bmat[:, 0], bmat[:, 1], wide(16), wide(17), t4)
            invert(0)
            nc.vector.reciprocal(rinv_col[:, 0:4], rinv_col[:, 0:4])
            order.done(nc.vector.reciprocal(rinv_col[0:NS, 4:5], rinv_col[0:NS, 4:5]))
            for a in range(AT):
                dve.wait_ge(block_done, a + 1)
                tt(halves(uT[:, a, :]), slot(a), halves(rinv[:, :]), ALU.mult).then_inc(evacuated, 1)
                if a < 3:
                    cmul(wtre[:, :, 2 - a, :], wtim[:, :, 2 - a, :], wtre[:, :, 3, :], wtim[:, :, 3, :],
                         wide(2 * a), wide(2 * a + 1), t4, wt_built if a == 2 else None)

            dve.wait_ge(evacuated, 4)
            dve.wait_ge(u_zeroed, 1)
            for q in range(4):
                rows = slice(GP * q, GP * (q + 1))
                for j in range(2, 4):
                    nc.vector.tensor_copy(
                        u2[GP * j:GP * (j + 1), :, :].rearrange("p (a q) c -> p a q c", q=4)[:, :, q, :],
                        uT[rows, :, 0:TP].rearrange("p a (c j) -> p a c j", j=CH)[:, :, :, j])
                ins = nc.vector.tensor_copy(
                    u_last[3 * GP:P, :, :].rearrange("p (a q) b -> p a q b", q=4)[:, :, q, :],
                    uT[rows, :, TP:T])
            ins.then_inc(u2_dve, 1)
            dve.wait_ge(kernel_done, 1)
            tt(dskip[3 * GP:P], aux[3 * GP:P, 0, :].rearrange("p (k g) -> p k g", k=PAIRS), dskip[3 * GP:P],
               ALU.add).then_inc(k0_added, 1)

            dve.wait_ge(mt_built, 1)
            nc.vector.memset(ere[:, :, 0:1], 1.0)
            order.done(nc.vector.memset(eim[:, :, 0:1], 0.0))
            s, pr, pi = 1, 20, 21
            while s < NCH:
                parts = 2 if s * PAIRS > 512 else 1
                n = PAIRS // parts
                for part in range(parts):
                    ks = slice(n * part, n * (part + 1))
                    t = [tmp[:, j, 0:n * s].rearrange("p (k c) -> p k c", k=n) for j in range(4)]
                    cmul(ere[:, ks, s:2 * s], eim[:, ks, s:2 * s], ere[:, ks, 0:s], eim[:, ks, 0:s],
                         v(pr)[:, ks].unsqueeze(2).broadcast_to([P, n, s]),
                         v(pi)[:, ks].unsqueeze(2).broadcast_to([P, n, s]), t)
                s *= 2
                if s < NCH:
                    nr, ni = (18, 19) if pr == 20 else (20, 21)
                    cmul(v(nr), v(ni), v(pr), v(pi), v(pr), v(pi), small)
                    pr, pi = nr, ni
            nc.vector.memset(sre3[:, :, 0:1], 0.0)
            order.done(nc.vector.memset(sim3[:, :, 0:1], 0.0))

            def project_read(n):
                dve.wait_ge(block_done, n + 1)
                if n < N_K:
                    stt(out=halves(qT[:, n - N_Q, :]), in0=slot(n), scalar=DH ** -0.5, in1=halves(rinv[:, :]),
                        op0=ALU.mult, op1=ALU.mult).then_inc(evacuated, 1)
                else:
                    tt(halves(kT[:, n - N_K, :]), slot(n), halves(rinv[:, :]), ALU.mult).then_inc(evacuated, 1)

            def pairs_of(e, b):
                return e[:, 4 * b:4 * b + 4, :].rearrange("p k c -> p (k c)")

            def scan(b):
                dve.wait_ge(v_done, b + 1)
                vr, vi = aux[:, 2 * (b % 2), :], aux[:, 2 * (b % 2) + 1, :]
                er, ei = pairs_of(ere, b), pairs_of(eim, b)
                t = [tmp[:, i, :] for i in range(4)]
                tt(t[0], vr, er, ALU.mult)
                tt(t[1], vi, ei, ALU.mult)
                tt(t[2], vi, er, ALU.mult)
                tt(t[3], vr, ei, ALU.mult).then_inc(v_read, 1)
                dve.wait_ge(v_read, b + 1)
                tt(t[0], t[0], t[1], ALU.add)
                order.done(tt(t[2], t[2], t[3], ALU.subtract))
                for r in range(4):
                    c = slice(NCH * r, NCH * (r + 1))
                    r4 = v(23)[:, 4 * b + r:4 * b + r + 1].broadcast_to([P, NCH])
                    nc.vector.tensor_tensor_scan(t[1][:, c], r4, t[0][:, c], 0.0, ALU.mult, ALU.add)
                    ins = nc.vector.tensor_tensor_scan(t[3][:, c], r4, t[2][:, c], 0.0, ALU.mult, ALU.add)
                order.done(ins)

            def turn_back(b):
                er, ei = pairs_of(ere, b), pairs_of(eim, b)
                t = [tmp[:, i, :] for i in range(4)]
                tw = [a.rearrange("p (k c) -> p k c", k=4) for a in t]
                out_re, out_im = (a[:, 4 * b:4 * b + 4, 1:NCH + 1] for a in (sre3, sim3))
                tt(t[0], t[1], er, ALU.mult)
                order.done(tt(t[2], t[3], ei, ALU.mult))
                order.done(tt(out_re, tw[0], tw[2], ALU.subtract))
                tt(t[0], t[1], ei, ALU.mult)
                order.done(tt(t[2], t[3], er, ALU.mult))
                tt(out_im, tw[0], tw[2], ALU.add).then_inc(states_done, 1)
                dve.wait_ge(states_done, b + 1)

            dve.wait_ge(u2_act, 1)
            for n in range(N_Q, N_V):
                project_read(n)
                if n >= N_Q + 1:
                    step = n - N_Q - 1
                    (scan if step % 2 == 0 else turn_back)(step // 2)
            turn_back(3)
            dve.wait_ge(vs_done, 1)
            lam1 = [v(i).unsqueeze(2).broadcast_to([P, PAIRS, NS]) for i in (0, 1)]
            h0s = [col(c, 0, PAIRS * NS).rearrange("p (k b) -> p k b", b=NS) for c in ("h0_re", "h0_im")]
            t = [tmp[:, i, 0:P].rearrange("p (k b) -> p k b", b=NS) for i in range(4)]
            out_re, out_im = ssm_out[:, 0, :, 0:NS], ssm_out[:, 1, :, 0:NS]
            cmul(out_re, out_im, h0s[0], h0s[1], lam1[0], lam1[1], t)
            for part, out in enumerate((out_re, out_im)):
                ins = tt(out, out, aux[:, 0, P * part:P * (part + 1)].rearrange("p (k b) -> p k b", b=NS), ALU.add)
            ins.then_inc(vs_read, 1)
            nc.vector.tensor_copy(ssm_out[:, 0, :, NS:NS + 1], sre3[:, :, NCH:NCH + 1]).then_inc(ssm_out_done, 1)
            nc.vector.tensor_copy(ssm_out[:, 1, :, NS:NS + 1], sim3[:, :, NCH:NCH + 1]).then_inc(ssm_out_done, 1)
            dve.wait_ge(vs_read, 1)
            for pair in range(2):
                dve.wait_ge(block_done, N_V + 2 * pair + 2)
                if pair == 1:
                    ts(vs, aux[0:NS, 1, :], rinv_col[0:NS, 4:5], None, ALU.mult).then_inc(vtail_read, 1)
                tt(vtok[:, :, 2 * P * pair:2 * P * (pair + 1)],
                   pj[:, 2 * pair:2 * pair + 2, :].rearrange("p b (t c) -> p (b t) c", t=2),
                   rinv_col[:, 0:4].unsqueeze(2).broadcast_to([P, 4, 2 * P]), ALU.mult).then_inc(evacuated, 2)

            dve.wait_ge(y_done, 5)
            order.done(nc.vector.memset(qbd[:, :, :, :], 0.0))
            nc.vector.tensor_copy(qbd[0:DH, :, :, 0], qT[0:DH, :, TP:T])
            nc.vector.tensor_copy(qbd[DH:P, :, :, 1], qT[DH:P, :, TP:T]).then_inc(qbd_ready, 1)
            order.done(ts(cap[:, :], col("sb_bias", 0, HEADS), -1.0, 40.0, ALU.mult, ALU.add))
            for a in range(AT):
                dve.wait_ge(y_hi_done, a + 1)
                tt(h_lo[:, AT + a, :], yT[:, a, :], h_hi[:, AT + a, :].bitcast(F32), ALU.subtract).then_inc(
                    y_split, 1)

            def read_pair(pair):
                dve.wait_ge(av_done, 2 * pair + 2)
                nc.vector.tensor_copy(osb[:, pair, 0:TP], o_bank(pair)).then_inc(o_read, 1)

            for h in range(HEADS):
                dve.wait_ge(qk_done, h + 1)
                if h >= 2:
                    dve.wait_ge(av_done, h - 1)
                for src, run in spans(h):
                    ins = ts(run, src, cap[:, h:h + 1], None, ALU.min)
                ins.then_inc(capped, 1)
                dve.wait_ge(soft_log, h + 1)
                for src, run in spans(h):
                    ins = stt(out=run, in0=src, scalar=col("sb_bias", h), in1=run, op0=ALU.add, op1=ALU.max)
                ins.then_inc(soft_done, 1)
                if h >= 3 and h % 2 == 1:
                    read_pair((h - 3) // 2)
                if 2 <= h < 6:
                    add_square(8 + h - 2, h == 2, 2 * MT, 1)
            read_pair(3)

            dve.wait_ge(dscore_pg, NS * PAGES)
            bias = col("sb_bias", 0, HEADS).unsqueeze(1).broadcast_to([P, PAGES * NS // 2, HEADS])
            dz4 = dz[:, 0, :].rearrange("p (a e h) -> p a e h", e=2, h=HEADS)
            for e, tensor in enumerate((pj, aux)):
                ins = tt(dz4[:, :, e, :], tensor[:, 2, 0:P].rearrange(
                    "p (a e h) -> p a e h", e=2, h=HEADS)[:, :, e, :], bias, ALU.add)
            order.done(ins)
            ts(dz[:, 1, :], dz[:, 0, :], 40.0, None, ALU.min).then_inc(dz_ready, 1)
            dve.wait_ge(dsoft_log, 1)
            tt(dz[:, 1, :], dz[:, 0, :], dz[:, 1, :], ALU.max).then_inc(dsp_ready, 1)
            invert(1, rinv_m[:, :])
            for kt in range(KT):
                stt(out=memx[:, kt, :], in0=memx[:, kt, :], scalar=col("g_mem_kv", kt), in1=rinv_m[:, :],
                    op0=ALU.mult, op1=ALU.mult).then_inc(m_scaled, 1)
            for m in range(AT):
                dve.wait_ge(sig_done, m + 1)
                tt(halves(yT[:, m, :]), slot(m), halves(yT[:, m, :]), ALU.mult).then_inc(evacuated, 1)
            dve.wait_ge(dcum_done, 1)
            tt(dz[:, 2, :], dz[:, 0, :], aux[:, 0, P:2 * P], ALU.add).then_inc(da_arg, 1)
            for kt in range(KT):
                dve.wait_ge(m_hi_done, kt + 1)
                tt(m_lo[:, kt, :], memx[:, kt, :], m_hi[:, kt, :].bitcast(F32), ALU.subtract).then_inc(m_split, 1)
            for a in range(AT):
                add_square(12 + a, a == 0, T, 2)
            dve.wait_ge(dav_pg, NS * PAGES)
            for t_ in range(PAGES):
                parts = aux[:, 1, P * t_:P * t_ + 2 * AT * NS].rearrange("p (b a e) -> p a b e", b=NS, a=AT)
                for e in range(2):
                    rows = slice(DH * e, DH * (e + 1))
                    if t_ == 0:
                        ins = nc.vector.tensor_copy(osb[rows, :, TP:T], parts[rows, :, :, e])
                    else:
                        ins = tt(osb[rows, :, TP:T], osb[rows, :, TP:T], parts[rows, :, :, e], ALU.add)
                if t_ == 0:
                    order.done(ins)
            ins.then_inc(dav_read, 1)
            invert(2)
            for a in range(AT):
                add_square(16 + a, a == 0, T, 3)
            for s in range(AT):
                stt(out=yT[:, s, :], in0=yT[:, s, :], scalar=col("g_ssm", s), in1=rinv[:, :],
                    op0=ALU.mult, op1=ALU.mult).then_inc(mix_scaled, 1)
            dve.wait_ge(kv_stored, 16 * 3)
            for n in range(N_MK, N_MV):
                dve.wait_ge(block_done, n + 1)
                nc.vector.tensor_copy(mkT[:, n - N_MK, :], slot(n)[:, 0, 0:MT]).then_inc(evacuated, 1)
            invert(3)
            for s in range(AT):
                stt(out=osb[:, s, :], in0=osb[:, s, :], scalar=col("g_sb", s), in1=rinv[:, :],
                    op0=ALU.mult, op1=ALU.mult).then_inc(mix_scaled, 1)
            for s in range(8):
                kt = (AT + s) % KT
                if s % 2 == 1:
                    pair = s // 2
                    dve.wait_ge(block_done, N_MV + s + 1)
                    nc.vector.tensor_copy(mv[:, :, 2 * P * pair:2 * P * (pair + 1)],
                                          pj[:, 2 * (pair % 2), :].rearrange("p (t c) -> p t c", t=2)
                                          ).then_inc(evacuated, 2)
                dve.wait_ge(h_hi_done, 8 + s + 1)
                src = yT if kt >= AT else osb
                tt(h_lo[:, kt, :], src[:, kt % AT, :], h_hi[:, kt, :].bitcast(F32), ALU.subtract).then_inc(h_split, 1)

            def residual(base, group, j0):
                for s in range(8):
                    dve.wait_ge(block_done, base + s + 1)
                    tt(halves(x[:, s, :]), slot(s), halves(x[:, s, :]), ALU.add).then_inc(evacuated, 1)
                    add_square(j0 + s, s == 0, T, group)

            def next_norm(group, gain, at_):
                split_low(0, gain, at_ + 1)
                split_low(1, gain, at_ + 2)
                invert(group)
                for kt in range(2, KT):
                    split_low(kt, gain, at_ + kt + 1)

            for part in range(2):
                nc.vector.memset(qz[part], 0.0)
            nc.vector.memset(pz, 0.0).then_inc(z_cleared, 1)
            dve.wait_ge(z_cleared, 1)

            residual(N_OUT, 4, 20)
            next_norm(4, "g_mem_q", 16)
            with dve.Fori(0, 2) as i:
                for s in range(4):
                    dve.wait_ge(block_done, N_MQ + s + 1 + i * 4)
                    stt(out=halves(qm[:, i * 4 + s, :]), in0=slot(s), scalar=(D // MH) ** -0.5,
                        in1=halves(rinv[:, :]), op0=ALU.mult, op1=ALU.mult).then_inc(evacuated, 1)
            dve.wait_ge(evacuated, N_MO + 2)
            for part in range(2):
                ins = nc.vector.tensor_copy(
                    qz[part].rearrange("p f (b w) -> p f b w", w=ROWS)[:, :, 0:NS, ROWS - 1],
                    qm[:, 4 * part:4 * part + 4, TP:T])
            ins.then_inc(qz_ready, 1)

            def mem_max(h):
                dve.wait_ge(s_done, h + 1)
                if h >= 2:
                    dve.wait_ge(p_ready, h - 1)
                banks = aux[:, 2 * (h % 2):2 * (h % 2) + 2, :].rearrange("p b (q k) -> p (b q) k", q=2)
                nc.vector.tensor_reduce(stat[:, h % 2, 0, :], banks, AX.X, ALU.max, negate=True).then_inc(
                    smax_done, 1)

            def mem_norm(h):
                dve.wait_ge(p_exp, 4 * (h + 1))
                order.done(nc.vector.reciprocal(stat[:, h % 2, 2, :], stat[:, h % 2, 1, :]))
                tt(prob[:, h % 2], prob[:, h % 2],
                   stat[:, h % 2, 2, :].unsqueeze(2).broadcast_to([P, 4, MT]), ALU.mult).then_inc(p_ready, 1)

            mem_max(0)
            mem_max(1)
            mem_norm(0)
            mem_norm(1)
            dve.wait_ge(kmd_used, NS)
            nc.vector.tensor_reduce(dstat[:, 0:1], pj[0:ROWS, 3, 0:MT], AX.X, ALU.max, negate=True).then_inc(
                drow_max, 1)
            dve.wait_ge(drow_exp, 1)
            order.done(nc.vector.reciprocal(dstat[:, 2:3], dstat[:, 1:2]))
            ts(drow[:, :], drow[:, :], dstat[:, 2:3], None, ALU.mult).then_inc(drow_ready, 1)
            for h in range(MH):
                if h + 2 < MH:
                    mem_max(h + 2)
                dve.wait_ge(o_hi, h + 1)
                tt(h_lo[:, 2 * h:2 * h + 2, 0:TP], pj[:, 2:4, :], h_hi[:, 2 * h:2 * h + 2, 0:TP].bitcast(F32),
                   ALU.subtract).then_inc(o_lo, 1)
                if h + 2 < MH:
                    mem_norm(h + 2)
            dve.wait_ge(do_hi, 1)
            tt(h_lo[:, :, TP:T].rearrange("p (h d) b -> p h d b", d=2),
               pj[:, 0, 0:2 * ROWS].rearrange("p (d b h) -> p h d b", d=2, h=MH),
               h_hi[:, :, TP:T].rearrange("p (h d) b -> p h d b", d=2).bitcast(F32),
               ALU.subtract).then_inc(do_lo, 1)

            residual(N_MO, 5, 28)
            next_norm(5, "g_ffn", 24)

            nc.vector.memset(gate[:, :, 0:2], 0.0).then_inc(gate_pads, 1)
            dve.wait_ge(gate_pads, 1)
            with order.loop(FT // 2, 4) as i:
                for c in range(2):
                    def tap(name):
                        return cols[:, bass.ds(i * 2 + (COL[name] + c), 1)]

                    def prev(r):
                        return cols[:, bass.ds(i * (4 * NS) + (COL["conv_prev"] + 2 * NS * c + NS * r), NS)]

                    dve.wait_ge(block_done, N_GU + 2 * c + 1 + i * 4)
                    tt(halves(gate[:, c, 2:T + 2]), slot(0), halves(rinv[:, :]), ALU.mult).then_inc(evacuated, 1)
                    dve.wait_ge(tap2_done, c + 1 + i * 2)
                    stt(out=conv[:, c, TP:T], in0=prev(1), scalar=tap("conv_w1"), in1=conv[:, c, TP:T],
                        op0=ALU.mult, op1=ALU.add)
                    order.done(stt(out=conv[:, c, 0:TP], in0=gate[:, c, 1:TP + 1], scalar=tap("conv_w1"),
                                   in1=conv[:, c, 0:TP], op0=ALU.mult, op1=ALU.add))
                    stt(out=conv[:, c, TP:T], in0=prev(0), scalar=tap("conv_w0"), in1=conv[:, c, TP:T],
                        op0=ALU.mult, op1=ALU.add)
                    stt(out=conv[:, c, 0:TP], in0=gate[:, c, 0:TP], scalar=tap("conv_w0"),
                        in1=conv[:, c, 0:TP], op0=ALU.mult, op1=ALU.add).then_inc(conv_done, 1)
                    dve.wait_ge(ff_gelu, c + 1 + i * 2)
                    order.done(tt(conv[:, c, :], conv[:, c, :], rinv[:, :], ALU.mult))
                    dve.wait_ge(block_done, N_GU + 2 * c + 2 + i * 4)
                    tt(halves(conv[:, c, :]), slot(1), halves(conv[:, c, :]), ALU.mult).then_inc(evacuated, 1)
                    dve.wait_ge(a_hi_done, c + 1 + i * 2)
                    tt(a_lo[:, i * 2 + c, :], conv[:, c, :], a_hi[:, i * 2 + c, :].bitcast(F32),
                       ALU.subtract).then_inc(a_split, 1)
            for m in range(KT):
                e = N_DOWN + 2 + m
                dve.wait_ge(block_done, N_DOWN + 3 * m + 3)
                tt(halves(x[:, m, :]), slot(e), halves(x[:, m, :]), ALU.add).then_inc(evacuated, 1)
                add_square(36 + m, m == 0, T, 6)
            invert(6)
            for kt in range(KT):
                stt(out=x[:, kt, :], in0=x[:, kt, :], scalar=col("g_final", kt), in1=rinv[:, :],
                    op0=ALU.mult, op1=ALU.mult).then_inc(y_scaled, 1)


def kernel(**inputs):
    import concourse.bacc as bacc
    from concourse.bass_utils import run_bass_kernel_spmd as run

    a = {k: np.asarray(v) for k, v in inputs.items()}
    f = np.float32

    def tiles(m):
        return m.T.reshape(-1, P, m.shape[0]).transpose(1, 0, 2)

    def column_block(w, c, width=P):
        b = w[:, c * width:(c + 1) * width].reshape(-1, P, width).transpose(1, 0, 2).reshape(P, -1)
        return np.pad(b, ((0, 0), (0, 1024 - b.shape[1])))

    w_in = a["w_in"][0]
    def half_blocks(w):
        return [column_block(w[D // 2 * part:D // 2 * (part + 1)], c, 2 * P)
                for c in range(w.shape[1] // (2 * P)) for part in range(2)]

    blocks = [column_block(w_in[:, o:o + SBW], c) for o in (3 * SBW, 0, SBW) for c in range(AT)]
    blocks += half_blocks(w_in[:, 2 * SBW:3 * SBW])
    blocks += [column_block(a["w_glu"][0], c, 2 * P) for c in range(2)]
    for name in ("w_mk", "w_mv", "w_out", "w_mq", "w_mo"):
        blocks += half_blocks(a[name][0]) if name == "w_mv" else [column_block(a[name][0], c) for c in range(KT)]
    for c in range(FT):
        blocks += [column_block(a[name][0], c) for name in ("w_gate", "w_up")]
    starts = [0, 8, 16, FT]
    for c in range(KT):
        blocks += [column_block(a["w_down"][0][P * starts[j]:P * starts[j + 1]], c) for j in range(3)]

    def vector(v):
        return v.reshape(-1, P).T

    def states(m):
        m = m.reshape((PAIRS, 2, 64) + m.shape[2:])
        return np.moveaxis(m, 0, 2).reshape((P, PAIRS) + m.shape[3:])

    conv_w = a["conv_w"][0]
    parts = dict(
        g_mix=vector(a["g_mix"][0]), g_mem_q=vector(a["g_mem_q"][0]), g_mem_kv=vector(a["g_mem_kv"][0]),
        g_ffn=vector(a["g_ffn"][0]), g_final=vector(a["g_final"]), g_sb=vector(a["g_sb_out"][0]),
        g_ssm=vector(a["g_ssm_out"][0]), b_glu=vector(a["b_glu"][0]),
        conv_w0=vector(conv_w[0]), conv_w1=vector(conv_w[1]), conv_w2=vector(conv_w[2]),
        conv_b=vector(a["conv_b"][0]),
        sb_bias=np.broadcast_to(a["sb_bias"][0], (P, HEADS)),
        lam_re=states(a["lam_re"][0]), lam_im=states(a["lam_im"][0]),
        log_dt=states(np.broadcast_to(a["log_dt"][0][:, None], (2 * PAIRS, 64))),
        h0_re=states(a["state_ssm_re"][0].transpose(1, 2, 0)).reshape(P, -1),
        h0_im=states(a["state_ssm_im"][0].transpose(1, 2, 0)).reshape(P, -1),
        conv_prev=a["state_conv"][0].reshape(NS, 2, FT, P).transpose(3, 2, 1, 0).reshape(P, -1))
    cols = np.concatenate([parts[k] for k in COL], axis=1)

    bc = np.zeros((P, 4, PAIRS, 2, 16), f)
    for i, m in enumerate((a["b_re"][0], a["b_im"][0], a["c_re"][0].transpose(0, 2, 1),
                           a["c_im"][0].transpose(0, 2, 1))):
        m = states(m)
        for g in range(2):
            bc[64 * g:64 * (g + 1), i, :, g] = m[64 * g:64 * (g + 1)]
    dskip = np.zeros((GP, PAIRS, GP), f)
    dskip[np.arange(GP), :, np.arange(GP)] = a["d_skip"][0].reshape(PAIRS, GP).T
    consts = np.stack([np.eye(P), -np.tril(np.ones((P, P))), -np.ones((P, P)), np.ones((P, P))], axis=1)

    kc, vc = a["cache_sb_k"][0], a["cache_sb_v"][0]
    km, vm = a["cache_mem_k"][0], a["cache_mem_v"][0]
    data = [
        tiles(np.concatenate([a["x_prompt"][0], a["x_sample"][:, 0]])),
        tiles(a["mem_prompt"][0]),
        np.stack(blocks), cols, bc.reshape(P, 4, PAIRS, GP), dskip, consts.astype(f),
        a["page_table"].reshape(1, -1),
        kc.reshape(-1, P, AT, P).transpose(0, 3, 2, 1).reshape(-1, P, SBW),
        vc.reshape(-1, P, SBW),
        km.reshape(NS, MT, KT, P).transpose(0, 3, 2, 1).reshape(NS, P, KT * MT),
        vm.reshape(NS, 2, P, D).transpose(0, 2, 1, 3).reshape(NS, P, 2 * D),
        a["state_conv"][0][:, 1],
    ]
    shapes = [(P, KT, T), (P, AT, T), (P, 4, SBW), (NS, SBW), (P, 2, PAIRS, NS + 1), (P, FT, 2 + NS), (NS, FF),
              (P, KT, MT), (P, 2, D)]

    nc = bacc.Bacc("TRN2", target_bir_lowering=False, num_devices=1)
    arrays, args = {}, []
    for i, m in enumerate(data):
        arrays[f"in_{i}"] = np.ascontiguousarray(m)
        args.append(nc.dram_tensor(f"in_{i}", m.shape, mybir.dt.from_np(m.dtype), kind="ExternalInput").ap())
    for i, shape in enumerate(shapes):
        args.append(nc.dram_tensor(f"out_{i}", shape, F32, kind="ExternalOutput").ap())
    build(nc, *args)
    r = run(nc, [arrays], core_ids=[0]).results[0]
    y, k, v, v_s, ssm, gate, conv_s0, mk, mv = (np.asarray(r[f"out_{i}"]) for i in range(len(shapes)))

    def rows(m):
        return m.transpose(2, 1, 0).reshape(m.shape[2], -1)

    y, k, gate = rows(y), rows(k), rows(gate)
    state = ssm.reshape(2, 64, 2, PAIRS, NS + 1).transpose(2, 4, 3, 0, 1).reshape(2, NS + 1, 2 * PAIRS, 64)
    return (y[None, :TP], y[TP:, None],
            k[:TP].reshape(1, 1, TP, HEADS, DH),
            v.transpose(1, 0, 2).reshape(1, 1, TP, HEADS, DH),
            state[0, NS][None, None], state[1, NS][None, None],
            gate[:2][None, None],
            rows(mk).reshape(1, 1, MT, MH, D // MH), mv.transpose(1, 0, 2).reshape(1, 1, MT, MH, D // MH),
            k[TP:].reshape(1, NS, 1, HEADS, DH), v_s.reshape(1, NS, 1, HEADS, DH),
            state[0, :NS][None], state[1, :NS][None],
            np.stack([conv_s0, gate[2:]], axis=1)[None])
```
